# Optimizing a Trainium2 kernel written in Bass

```python
import jax, jax.numpy as jnp
from jax import lax
import numpy as np

D_MODEL = 1024
BATCH = 1
SEQ = 256
DEPTH = 1

N_MEM = 256
MEM_HEADS = 4
MEM_HEAD_DIM = 128
MEM_WIDTH = MEM_HEADS * MEM_HEAD_DIM
GDN_HEADS = 4
GDN_HEAD_DIM = 128
GDN_WIDTH = GDN_HEADS * GDN_HEAD_DIM
GDN_CONV = 4
GDN_CHUNK = 64
CONV_WIDTH = 512
SHORT_CONV = 3
N_BRANCH = 3
N_EXPERTS = 32
TOP_K = 4
D_FF_EXPERT = 1024
SWIGLU_LIMIT = 7.0
SWIGLU_ALPHA = 1.702
MOE_BLOCK = 256
LN_EPS = 1e-5
RMS_EPS = 1e-6
DEEPNORM_ALPHA = (2 * DEPTH) ** 0.25
DEEPNORM_BETA = (8 * DEPTH) ** -0.25

IN_SPLIT_SIZES = (3 * GDN_WIDTH, GDN_HEADS, GDN_HEADS, GDN_WIDTH,
                  CONV_WIDTH, CONV_WIDTH, CONV_WIDTH, MEM_WIDTH, N_BRANCH * D_MODEL)
D_IN_PROJ = 3 * GDN_WIDTH + 2 * GDN_HEADS + GDN_WIDTH + 3 * CONV_WIDTH + MEM_WIDTH + N_BRANCH * D_MODEL

kernel_name = 'hybrid_gdn_shortconv_memxattn_moe_deepnorm'

def layer_norm(x, g, b):
    xf = x.astype(jnp.float32)
    mu = jnp.mean(xf, axis=-1, keepdims=True)
    var = jnp.mean(jnp.square(xf - mu), axis=-1, keepdims=True)
    y = (xf - mu) * lax.rsqrt(var + LN_EPS) * g.astype(jnp.float32) + b.astype(jnp.float32)
    return y.astype(x.dtype)

def l2_normalize(x):
    return x * lax.rsqrt(jnp.sum(jnp.square(x), axis=-1, keepdims=True) + RMS_EPS)

def causal_depthwise_conv(x, w):
    k_w = w.shape[0]
    return lax.conv_general_dilated(
        x, w[:, None, :].astype(x.dtype), window_strides=(1,), padding=[(k_w - 1, 0)],
        dimension_numbers=('NWC', 'WIO', 'NWC'), feature_group_count=x.shape[-1])

def gated_delta_rule_chunked(q, k, v, g, beta):
    b_, h_, t_, dk = q.shape
    dv = v.shape[-1]
    nc = t_ // GDN_CHUNK

    def chunks(t):
        return t.reshape(b_, h_, nc, GDN_CHUNK, *t.shape[3:])

    q, k, v, g, beta = chunks(q), chunks(k), chunks(v), chunks(g), chunks(beta)
    g_cum = jnp.cumsum(g, axis=-1)
    pos = jnp.arange(GDN_CHUNK)
    causal = pos[:, None] >= pos[None, :]
    strict = pos[:, None] > pos[None, :]
    decay = jnp.exp(jnp.where(causal, g_cum[..., :, None] - g_cum[..., None, :], -jnp.inf))
    k_beta = k * beta[..., None]
    kk = jnp.where(strict, jnp.einsum('bhnid,bhnjd->bhnij', k_beta, k) * decay, 0.0)
    rhs = jnp.concatenate([v * beta[..., None], k_beta * jnp.exp(g_cum)[..., None]], axis=-1)
    sol = lax.linalg.triangular_solve(kk + jnp.eye(GDN_CHUNK, dtype=kk.dtype), rhs,
                                      left_side=True, lower=True, unit_diagonal=True)
    u, k_cum = sol[..., :dv], sol[..., dv:]
    qk = jnp.einsum('bhnid,bhnjd->bhnij', q, k) * decay
    q_dec = q * jnp.exp(g_cum)[..., None]
    k_end = k * jnp.exp(g_cum[..., -1:] - g_cum)[..., None]
    chunk_dec = jnp.exp(g_cum[..., -1])

    def step(state, inp):
        u_c, kc_c, qk_c, qd_c, ke_c, cd_c = inp
        v_new = u_c - jnp.einsum('bhcd,bhde->bhce', kc_c, state)
        o_c = jnp.einsum('bhcd,bhde->bhce', qd_c, state) + jnp.einsum('bhij,bhje->bhie', qk_c, v_new)
        state = state * cd_c[..., None, None] + jnp.einsum('bhcd,bhce->bhde', ke_c, v_new)
        return state, o_c

    xs = tuple(jnp.moveaxis(t, 2, 0) for t in (u, k_cum, qk, q_dec, k_end, chunk_dec))
    s0 = jnp.zeros((b_, h_, dk, dv), jnp.float32)
    _, o = lax.scan(step, s0, xs)
    return jnp.moveaxis(o, 0, 2).reshape(b_, h_, t_, dv)

def token_mixer(x, mem, w_in, conv_qkv, conv_mix, a_log, dt_bias, gdn_norm, w_mem_kv, w_br, w_o):
    b_, t_, _ = x.shape
    f32 = jnp.float32
    split_idx = np.cumsum(IN_SPLIT_SIZES)[:-1].tolist()
    proj = x @ w_in
    qkv, a, bt, z, xc, gb, gc, qm, gl = jnp.split(proj, split_idx, axis=-1)

    qkv = jax.nn.silu(causal_depthwise_conv(qkv, conv_qkv)).astype(f32)
    q, k, v = jnp.split(qkv, 3, axis=-1)

    def heads(t):
        return t.reshape(b_, t_, GDN_HEADS, GDN_HEAD_DIM).transpose(0, 2, 1, 3)

    q = l2_normalize(heads(q)) * (GDN_HEAD_DIM ** -0.5)
    k = l2_normalize(heads(k))
    v = heads(v)
    g = -(jnp.exp(a_log.astype(f32)) * jax.nn.softplus(a.astype(f32) + dt_bias.astype(f32)))
    g = g.transpose(0, 2, 1)
    beta = jax.nn.sigmoid(bt.astype(f32)).transpose(0, 2, 1)
    o = gated_delta_rule_chunked(q, k, v, g, beta).transpose(0, 2, 1, 3)
    o = o * lax.rsqrt(jnp.mean(jnp.square(o), axis=-1, keepdims=True) + RMS_EPS) * gdn_norm.astype(f32)
    zz = z.reshape(b_, t_, GDN_HEADS, GDN_HEAD_DIM).astype(f32)
    y_a = (o * jax.nn.silu(zz)).reshape(b_, t_, GDN_WIDTH).astype(x.dtype)

    y_b = gb * causal_depthwise_conv(gc * xc, conv_mix)

    kv = mem @ w_mem_kv
    km, vm = jnp.split(kv, 2, axis=-1)
    qh = qm.reshape(b_, t_, MEM_HEADS, MEM_HEAD_DIM)
    km = km.reshape(b_, -1, MEM_HEADS, MEM_HEAD_DIM)
    vm = vm.reshape(b_, -1, MEM_HEADS, MEM_HEAD_DIM)
    s = jnp.einsum('bthd,bmhd->bhtm', qh, km).astype(f32) * (MEM_HEAD_DIM ** -0.5)
    p = jax.nn.softmax(s, axis=-1).astype(x.dtype)
    y_m = jnp.einsum('bhtm,bmhd->bthd', p, vm).reshape(b_, t_, MEM_WIDTH)

    gates = jax.nn.sigmoid(gl.reshape(b_, t_, N_BRANCH, D_MODEL))
    merged = (gates[:, :, 0] * (y_a @ w_br[0])
              + gates[:, :, 1] * (y_b @ w_br[1])
              + gates[:, :, 2] * (y_m @ w_br[2]))
    return merged @ w_o

def moe_ffn(x, w_router, b_router, w_gate_up, b_gate_up, w_down, b_down):
    b_, t_, d_ = x.shape
    n_tok = b_ * t_
    xt = x.reshape(n_tok, d_)
    logits = (xt @ w_router + b_router).astype(jnp.float32)
    top_logits, top_idx = lax.top_k(logits, TOP_K)
    top_w = jax.nn.softmax(top_logits, axis=-1).astype(x.dtype)
    n_assign = n_tok * TOP_K
    flat_e = top_idx.reshape(n_assign)
    flat_tok = jnp.arange(n_assign, dtype=jnp.int32) // TOP_K
    flat_w = top_w.reshape(n_assign)
    order = jnp.argsort(flat_e)
    sorted_e = flat_e[order]
    counts = jnp.bincount(flat_e, length=N_EXPERTS)
    padded = (counts + MOE_BLOCK - 1) // MOE_BLOCK * MOE_BLOCK
    pad_end = jnp.cumsum(padded)
    pad_start = pad_end - padded
    start = jnp.cumsum(counts) - counts
    dest = pad_start[sorted_e] + jnp.arange(n_assign, dtype=jnp.int32) - start[sorted_e]
    n_blocks = (n_assign + N_EXPERTS * (MOE_BLOCK - 1) + MOE_BLOCK - 1) // MOE_BLOCK
    n_slots = n_blocks * MOE_BLOCK
    slot_tok = jnp.zeros((n_slots,), jnp.int32).at[dest].set(flat_tok[order])
    slot_w = jnp.zeros((n_slots,), x.dtype).at[dest].set(flat_w[order])
    block_e = jnp.minimum(jnp.searchsorted(pad_end, jnp.arange(n_blocks) * MOE_BLOCK, side='right'),
                          N_EXPERTS - 1)

    def expert_block(args):
        tok, wgt, e = args
        xb = xt[tok]
        gu = xb @ w_gate_up[e] + b_gate_up[e]
        gate, up = jnp.split(gu, 2, axis=-1)
        gate = jnp.minimum(gate, SWIGLU_LIMIT)
        up = jnp.clip(up, -SWIGLU_LIMIT, SWIGLU_LIMIT)
        h = (up + 1.0) * (gate * jax.nn.sigmoid(gate * SWIGLU_ALPHA))
        return (h @ w_down[e] + b_down[e]) * wgt[:, None]

    ys = lax.map(expert_block, (slot_tok.reshape(n_blocks, MOE_BLOCK),
                                slot_w.reshape(n_blocks, MOE_BLOCK), block_e))
    out = jax.ops.segment_sum(ys.reshape(n_slots, d_), slot_tok, num_segments=n_tok)
    return out.reshape(b_, t_, d_)

def setup_inputs(seed: int = 0) -> dict:
    key = jax.random.key(seed)
    ks = jax.random.split(key, 24)
    f32 = jnp.float32
    L = DEPTH

    def nrm(k, shape, scale):
        return jax.random.normal(k, shape, f32) * scale

    dt = jnp.exp(jax.random.uniform(ks[7], (L, GDN_HEADS), f32, float(np.log(1e-3)), float(np.log(1e-1))))
    return {
        'x': nrm(ks[0], (BATCH, SEQ, D_MODEL), 1.0),
        'mem': nrm(ks[1], (BATCH, N_MEM, D_MODEL), 1.0),
        'ln0_g': 1.0 + nrm(ks[2], (D_MODEL,), 0.02),
        'ln0_b': nrm(ks[3], (D_MODEL,), 0.02),
        'w_in': nrm(ks[4], (L, D_MODEL, D_IN_PROJ), D_MODEL ** -0.5),
        'conv_qkv': nrm(ks[5], (L, GDN_CONV, 3 * GDN_WIDTH), GDN_CONV ** -0.5),
        'conv_mix': nrm(ks[6], (L, SHORT_CONV, CONV_WIDTH), SHORT_CONV ** -0.5),
        'a_log': jnp.log(jax.random.uniform(ks[8], (L, GDN_HEADS), f32, 1.0, 16.0)),
        'dt_bias': dt + jnp.log(-jnp.expm1(-dt)),
        'gdn_norm': 1.0 + nrm(ks[9], (L, GDN_HEAD_DIM), 0.02),
        'w_mem_kv': nrm(ks[10], (L, D_MODEL, 2 * MEM_WIDTH), D_MODEL ** -0.5),
        'w_br': nrm(ks[11], (L, N_BRANCH, GDN_WIDTH, D_MODEL), GDN_WIDTH ** -0.5),
        'w_o': nrm(ks[12], (L, D_MODEL, D_MODEL), DEEPNORM_BETA * D_MODEL ** -0.5),
        'ln1_g': 1.0 + nrm(ks[13], (L, D_MODEL), 0.02),
        'ln1_b': nrm(ks[14], (L, D_MODEL), 0.02),
        'w_router': nrm(ks[15], (L, D_MODEL, N_EXPERTS), D_MODEL ** -0.5),
        'b_router': nrm(ks[16], (L, N_EXPERTS), 0.01),
        'w_gate_up': nrm(ks[17], (L, N_EXPERTS, D_MODEL, 2 * D_FF_EXPERT), D_MODEL ** -0.5),
        'b_gate_up': nrm(ks[18], (L, N_EXPERTS, 2 * D_FF_EXPERT), 0.01),
        'w_down': nrm(ks[19], (L, N_EXPERTS, D_FF_EXPERT, D_MODEL), DEEPNORM_BETA * D_FF_EXPERT ** -0.5),
        'b_down': nrm(ks[20], (L, N_EXPERTS, D_MODEL), 0.01),
        'ln2_g': 1.0 + nrm(ks[21], (L, D_MODEL), 0.02),
        'ln2_b': nrm(ks[22], (L, D_MODEL), 0.02),
    }

def reference(x, mem, ln0_g, ln0_b, w_in, conv_qkv, conv_mix, a_log, dt_bias, gdn_norm,
              w_mem_kv, w_br, w_o, ln1_g, ln1_b, w_router, b_router, w_gate_up, b_gate_up,
              w_down, b_down, ln2_g, ln2_b):
    h = layer_norm(x, ln0_g, ln0_b)
    for l in range(DEPTH):
        mix = token_mixer(h, mem, w_in[l], conv_qkv[l], conv_mix[l], a_log[l], dt_bias[l],
                          gdn_norm[l], w_mem_kv[l], w_br[l], w_o[l])
        h = layer_norm(DEEPNORM_ALPHA * h + mix, ln1_g[l], ln1_b[l])
        ffn = moe_ffn(h, w_router[l], b_router[l], w_gate_up[l], b_gate_up[l], w_down[l], b_down[l])
        h = layer_norm(DEEPNORM_ALPHA * h + ffn, ln2_g[l], ln2_b[l])
    return h


_drawn_inputs = setup_inputs


def setup_inputs(seed=0):
    import zlib

    import numpy as np

    out = dict(_drawn_inputs(seed))
    spreads = {}
    factors = {'gdn_norm': 4.293,
     'b_router': 2.933,
     'b_gate_up': 8.0,
     'b_down': 8.0,
     'ln2_g': 2.751,
     'ln2_b': 2.828}
    for name, (base, spread) in spreads.items():
        noise = np.random.default_rng([zlib.crc32(name.encode()), seed]).standard_normal(out[name].shape)
        drawn = base * np.exp(spread * noise) if base else spread * noise
        out[name] = __import__('jax').numpy.asarray(drawn.astype(out[name].dtype))
    for name, factor in factors.items():
        out[name] = (out[name] * factor).astype(out[name].dtype)
    return out
```

```python
from contextlib import ExitStack

import concourse.bass as bass
from concourse import mybir

F32 = mybir.dt.float32
F32R = mybir.dt.float32r
I32 = mybir.dt.int32
U32 = mybir.dt.uint32
BF16 = mybir.dt.bfloat16
ALU = mybir.AluOpType
ACT = mybir.ActivationFunctionType
AX = mybir.AxisListType

P = 128
D = 1024
T = 256
NT = T // P
KD = D // P
H = 4
DH = 128
W = H * DH
NMEM = 256
CHUNK = 64
NPB = NT * H
LEVELS = 6
NE = 32
TOPK = 4
FF = 1024
CAP = 64
EXTRA = T * TOPK // CAP
ITEMS = NE + EXTRA + 1
SLOT = 4096
RAW = 3
PIECE = SLOT // 4
SPLITS = 3
EC = 6
RING = 10
ROUND = 5
ROUNDS = (NE - 2) // ROUND
assert ROUND * EC % RING == 0 and ROUNDS * ROUND == NE - 2
LN_EPS = 1e-5
RMS_EPS = 1e-6
ALPHA = 2 ** 0.25
LIMIT = 7.0
SWIGLU_ALPHA = 1.702
NOT_HERE = 1000.0
BIG = 1e30

C_QKV, C_AB = 0, 3 * W
C_Z = C_AB + 2 * H
C_XC, C_GB, C_GC, C_QM = C_Z + W, C_Z + 2 * W, C_Z + 3 * W, C_Z + 4 * W
C_GL = C_Z + 5 * W

MIXER_SLOTS = (
    [("kv", 0), ("kv", W)]
    + [("in", C_QKV + W * n) for n in range(3)]
    + [("in", c) for c in (C_Z, C_XC, C_GC, C_GB, C_QM)]
    + [s for b in (2, 1, 0) for s in (("in", C_GL + D * b), ("in", C_GL + D * b + W), ("br", b))]
    + [("wo", 0), ("wo", W)]
)
N_MIX = len(MIXER_SLOTS)

GDN_STEPS = (
    ["scalars", "decay", "norms", "scores", "tokens"]
    + [f"{half}{n}" for n in range(LEVELS) for half in ("lx", "xlx")]
    + ["kcum"]
    + [f"{half}{n}" for n in range(T // CHUNK) for half in ("vnew", "state")]
    + ["onorm"]
)


def mixer_schedule():
    order = [("memT", n) for n in range(4)]
    order += [("km", 0), ("ln", 0, 0), ("km", 1), ("ln", 0, 1), ("km", 2), ("km", 3)]
    order += [("hT", t, j) for t in range(NT) for j in range(2)] + [("ab", 0)]
    order += [("vm", n) for n in range(NT)]
    order += [("qkv", n) for n in range(5)] + [("g", "scalars")]
    order += [("qkv", n) for n in range(5, 9)] + [("g", "decay")]
    order += [("qkv", n) for n in range(9, 12)]
    attention = [("score", 0), ("score", 1), ("score", 2), ("score", 3), ("pT", 0), ("pT", 1), ("ym", 0),
                 ("pT", 2), ("ym", 1), ("pT", 3), ("ym", 2), ("ym", 3)]
    long = [(kind, n) for kind in ("z", "xc", "gc", "gb", "qm") for n in range(4)]
    g = [s for s in GDN_STEPS if s not in ("scalars", "decay")]
    for unit in long:
        order += [unit, ("g", g.pop(0))]
    for n in range(KD):
        order += [("gate", 2, n)] + ([("g", g.pop(0))] if g else [])
        order += attention[:2] if n < 6 else []
        attention = attention[2:]
    assert not g and not attention
    for b in (2, 1, 0):
        order += [("gate", b, n) for n in range(KD)] if b < 2 else []
        for n in range(KD):
            order += [("br", b, n)] + ([("sum", n)] if b == 0 else [])
        order += [("ya", 0)] if b == 2 else []
    for n in range(2):
        order += [("wo", n, t) for t in range(NT)]
    for t in range(NT):
        order += [("ln", 1, t)] + [("x1T", t, j) for j in range(2)] + [("logits", t)]
    order += [("rank", 0)]
    out, q = [("prep", n) for n in range(SPLITS)], 0
    uses = {}
    for s in order:
        n = {"km": 1, "qkv": 1, "z": 1, "xc": 1, "gc": 1, "gb": 1, "qm": 1, "gate": 1}.get(s[0], 0)
        if s[0] == "br":
            n = s[2] % 2
            uses[s] = [q]
        if s[0] in ("vm", "wo"):
            n = 4 * (s[-1] == 0)
        if n:
            uses[s] = list(range(q, q + n))
            out += [("prep", m + SPLITS) for m in uses[s] if m + SPLITS < 4 * N_MIX]
            q += n
        out.append(s)
    assert q == 4 * N_MIX
    return out, uses


SCHEDULE, PIECES_OF = mixer_schedule()
NOT_UNITS = ("g", "prep", "ln", "ya", "sum")
UNITS = [s for s in SCHEDULE if s[0] not in NOT_UNITS]
BANKS = 3


def hybrid_layer(nc, x, mem, ln0_g, ln0_b, w_in, conv_qkv, conv_mix, a_log, dt_bias, gdn_norm,
                 w_mem_kv, w_br, w_o, ln1_g, ln1_b, w_router, b_router, w_gate_up, b_gate_up,
                 w_down, b_down, ln2_g, ln2_b, out):
    with ExitStack() as ctx:
        def sb(name, shape, dt=F32, scope=ctx):
            return scope.enter_context(nc.sbuf_tensor(name, shape, dt))

        def sem(name):
            return ctx.enter_context(nc.semaphore(name))

        ps = [ctx.enter_context(nc.psum_tensor(f"bank{n}", [P, 512], F32)) for n in range(8)]

        class Space:

            def __init__(self, tensor, size):
                self.tensor, self.size, self.used = tensor, size, 0

            def at(self, start, *shape):
                n = 1
                for k in shape:
                    n *= k
                assert start + n <= self.size, (start + n, self.size)
                a = self.tensor[:, start:start + n]
                if len(shape) == 2:
                    a = a.rearrange("p (a b) -> p a b", b=shape[1])
                return a

            def new(self, *shape):
                a, n = self.at(self.used, *shape), 1
                for k in shape:
                    n *= k
                self.used += n
                return a

        hx = sb("hx", [P, NT, D])
        raw = sb("raw", [P, RAW, SLOT])
        wr = sb("wr", [P, KD, NE])
        br_bc = sb("br_bc", [P, NE])
        ident = sb("ident", [P, P])
        ones = sb("ones", [P, P])
        block_upper = sb("block_upper", [P, P])
        block_ones = sb("block_ones", [P, P])
        negmask = sb("negmask", [P, P])
        before = sb("before", [P, P])
        level_mask = sb("level_mask", [P, LEVELS, P], BF16)
        small_rows = sb("small_rows", [64, P])
        small_cols = sb("small_cols", [P, 64])
        w_ab = sb("w_ab", [P, KD, 2 * H])
        w_ab_hi = sb("w_ab_hi", [P, KD, 2 * H], F32R)
        w_ab_lo = sb("w_ab_lo", [P, KD, 2 * H], F32R)
        adt = sb("adt", [P, 2, H])
        top_i = sb("top_i", [P, NT, 8], U32)
        ids_i = sb("ids_i", [1, ITEMS], I32)
        count_i = sb("count_i", [1, 1], I32)
        tiny = Space(sb("tiny", [P, 188]), 188)
        ln_stats = [[tiny.new(6) for _ in range(2)] for _ in range(NT)]
        ln_mv, ln_std, ln_rstd = tiny.new(NT, 2), tiny.new(NT), tiny.new(NT)
        eps_ln, eps_rms = tiny.new(1), tiny.new(1)
        pre_g, beta = tiny.new(NT, H), tiny.new(NT, H)
        t_a, t_b, t_c = tiny.new(NT, H), tiny.new(NT, H), tiny.new(NT, H)
        g_log, ea = tiny.new(NT, H), tiny.new(H)
        gcum, bexp, kend_s = tiny.new(NT, H), tiny.new(NT, H), tiny.new(NT, H)
        chunk_decay = tiny.new(NPB, 2)
        s_max, s_neg, s_sum, s_rec = (tiny.new(H, NT) for _ in range(4))
        o_ss, o_rs = tiny.new(NPB), tiny.new(NPB)

        early = ExitStack()
        EARLY = 22000
        e = Space(sb("early", [P, EARLY], scope=early), EARLY)
        R = 1024
        o_pad = e.used; qkv_pad = e.new(12, T + 3)
        squares = e.at(o_pad, 2 * H, T)
        T1, LTs = e.at(o_pad, NPB, P), [e.at(o_pad + R, NPB, P), e.at(o_pad + 2 * R, NPB, P)]
        nkcT, o_tok = e.at(o_pad, H, T), e.at(o_pad + R, NT, W)
        o_qkv = e.used; qkvT = e.new(12, T)
        blocks = e.at(o_qkv, LEVELS + 1, P)
        qT, kT, vT = qkvT[:, 0:H, :], qkvT[:, H:2 * H, :], qkvT[:, 2 * H:3 * H, :]
        kbe, vbeta = e.at(o_qkv + R, NPB, P), e.at(o_qkv + 2 * R, NPB, P)
        decayT_o = e.used; decayT = e.new(NPB, P)
        yaT = e.at(decayT_o, H, T)
        o_eb = e.used; expg = e.new(NPB, P)
        state, vnew = e.at(o_eb, H, DH), e.at(o_eb + W, H, DH)
        LT = e.new(NPB, P)
        kend = e.new(NPB, P)
        o_gb = e.used + H * T
        zs, gb, xc, qm = (e.new(H, T) for _ in range(4))
        first_gates = e.at(o_gb, KD, T)
        kmT, vm = e.new(H, NMEM), e.new(NT, W)
        upad_o = e.used; upad = e.new(H, T + 2)
        pT = e.at(upad_o, H, T)
        DEAD = e.used
        o_x = e.used; X, XT = e.new(NPB, P), e.new(NPB, P)
        lnp0 = e.at(o_x, 2, D)
        merged = e.at(o_x, KD, T)
        o_mem = e.used; mem_tok = e.new(NT, D)
        g_rows, beta_rows = e.at(o_mem, NPB, P), e.at(o_mem + R, NPB, P)
        probs = e.at(o_mem, H, 2 * T).rearrange("p h (t m) -> p h t m", t=NT)
        gates = e.at(o_mem, KD, T)
        GATED = e.used
        act_hi, act_lo = (sb(n, [P, KD, T], F32R, early) for n in ("act_hi", "act_lo"))
        src_hi, src_lo = (sb(n, [P, KD, T], F32R, early) for n in ("src_hi", "src_lo"))
        w_hi, w_lo = (sb(n, [P, SPLITS, PIECE], F32R, early) for n in ("w_hi", "w_lo"))
        early.close()

        LATE = 36700
        l = Space(sb("late", [P, LATE]), LATE)
        first_slots = [l.new(SLOT) for _ in range(3)]
        bgu, bdown = l.new(2 * FF), l.new(D)
        lnp1 = l.new(2, D)
        assert l.used <= DEAD
        x_slotT = l.new(KD, CAP)
        up1, gate1 = l.new(512), l.new(512)
        h_tok = gate1
        slot_iota, part_iota, e_iota = l.new(P), l.new(P), l.new(NE)
        e_row = l.new(CAP)
        onehot, onehot_w = l.new(NT, CAP), l.new(NT, P)
        ranks, weights, ids = l.new(NT, ITEMS), l.new(NT, ITEMS), l.new(ITEMS)
        logits, el, mask = l.new(NT, NE), l.new(NT, NE), l.new(NT, NE)
        top_v, top_f, top_e = l.new(NT, 8), l.new(NT, 8), l.new(NT, 8)
        r_neg, r_sum, r_rec = l.new(NT), l.new(NT), l.new(NT)
        q16, sel, selb = l.new(EXTRA), l.new(EXTRA), l.new(EXTRA)
        cnt, ext, ext2 = l.new(1), l.new(1), l.new(1)
        assert l.used <= GATED, (l.used, GATED)
        hidT = lnp1[:, 0, 0:512].rearrange("p (a b) -> p a b", b=P)
        y_tok = lnp1[:, 0, 512:1024]
        scatter = lnp1[:, 1, 0:T]
        weightT = lnp1[:, 1, T:2 * T]
        sig1 = lnp1[:, 1, 512:1024]
        rankT = sig1[:, 0:T]
        late_slots = [l.new(SLOT) for _ in range(4)]
        x1T = l.at(l.used - KD * T, KD, T)

        RING_SLOTS = [raw[:, n, :] for n in range(RAW)] + first_slots + late_slots
        assert len(RING_SLOTS) == RING
        LN2_SLOT = RAW
        LAST_IN_LN2_SLOT = max(m for m in range(NE * EC) if m % RING == LN2_SLOT)
        assert LAST_IN_LN2_SLOT < (NE - 1) * EC
        lnp2 = RING_SLOTS[LN2_SLOT][:, 0:2 * D].rearrange("p (a b) -> p a b", a=2)

        x_in, mem_in = sem("x_in"), sem("mem_in")
        rows_in, ab_in, adt_in = sem("rows_in"), sem("ab_in"), sem("adt_in")
        lnp_in = [sem(f"lnp{n}_in") for n in range(3)]
        router_in, ebias_in = sem("router_in"), sem("ebias_in")
        raw_in = [sem(f"raw_in{n}") for n in range(RAW)]
        first_in = [sem(f"first_in{n}") for n in range(3)]
        late_in = [sem(f"late_in{n}") for n in range(4)]
        split_hi = sem("split_hi")
        split_lo = {"dve": sem("split_lo_dve"), "pool": sem("split_lo_pool")}
        joint_piece = sem("joint_piece")
        bank_full = [sem(f"bank_full{n}") for n in range(BANKS)]
        bank_free = [sem(f"bank_free{n}") for n in range(BANKS)]
        bank_hi = sem("bank_hi")
        consts, pads = sem("consts"), sem("pads")
        cols_turned, cols_ready = sem("cols_turned"), sem("cols_ready")
        pool_chain, dve_chain, act_chain = sem("pool_chain"), sem("dve_chain"), sem("act_chain")
        ln_var, ln_root, ln_done = sem("ln_var"), sem("ln_root"), sem("ln_done")
        conv_done, silu_done = sem("conv_done"), sem("silu_done")
        g_pe, g_dve, g_act, g_pool = sem("g_pe"), sem("g_dve"), sem("g_act"), sem("g_pool")
        ab_split, ab_act, ab_dve = sem("ab_split"), sem("ab_act"), sem("ab_dve")
        g_dve_scal, g_dve_sq = sem("g_dve_scal"), sem("g_dve_sq")
        att_max, att_p = sem("att_max"), sem("att_p")
        gate_used = sem("gate_used")
        yb_ready, yb_hi, yb_split = sem("yb_ready"), sem("yb_hi"), sem("yb_split")
        ya_ready, ya_hi, ya_split = sem("ya_ready"), sem("ya_hi"), sem("ya_split")
        sum_ready, sum_hi, sum_split = sem("sum_ready"), sem("sum_hi"), sem("sum_split")
        r_max, r_exp, r_mask, r_ext, r_counted, r_sel, r_cols, r_items = (sem(n) for n in (
            "r_max", "r_exp", "r_mask", "r_ext", "r_counted", "r_sel", "r_cols", "r_items"))
        moe_consts = sem("moe_consts")
        onehots, gathered, tokens_in = sem("onehots"), sem("gathered"), sem("tokens_in")
        chunks_used = sem("chunks_used")
        gu_done, gate_cut, sig_done, hid_done = sem("gu_done"), sem("gate_cut"), sem("sig_done"), sem("hid_done")
        up_cut, up_gate = sem("up_cut"), sem("up_gate")
        hid_turned, hid_copied = sem("hid_turned"), sem("hid_copied")
        down_done, y_copied = sem("down_done"), sem("y_copied")
        sc_turned, sc_copied, item_done = sem("sc_turned"), sem("sc_copied"), sem("item_done")
        out_stored = sem("out_stored")

        unit_at = {u: n for n, u in enumerate(UNITS)}

        def bank_of(u):
            return unit_at[u] % BANKS

        def turn_of(u):
            return unit_at[u] // BANKS + 1

        piece_end, joint = {}, 0
        for u in UNITS:
            for q in PIECES_OF.get(u, []):
                if len(PIECES_OF[u]) == 4 and q < PIECES_OF[u][3]:
                    joint += 1
                    piece_end[q] = (joint_piece, joint)
                else:
                    v = u[:-1] + (1,) if u[0] in ("vm", "wo") else u
                    piece_end[q] = (bank_full[bank_of(v)], turn_of(v))

        def lo_engine(q):
            return "pool" if q % 2 == 0 else "dve"

        def piece_views(q):
            n, j = q // 4, q % 4
            kind = MIXER_SLOTS[n][0]
            flat, hi, lo = raw[:, n % RAW, :], w_hi[:, q % SPLITS, :], w_lo[:, q % SPLITS, :]
            if kind == "br":
                k, src = H, flat.rearrange("p (k n) -> p k n", k=H)[:, :, 2 * P * j:2 * P * (j + 1)]
            elif MIXER_SLOTS[n] == ("kv", W) or kind == "wo":
                k, src = 2, flat.rearrange("p (k n) -> p k n", k=KD)[:, 2 * j:2 * j + 2, :]
            else:
                k, src = KD, flat.rearrange("p (k n) -> p k n", k=KD)[:, :, P * j:P * (j + 1)]
            return src, hi.rearrange("p (k n) -> p k n", k=k), lo.rearrange("p (k n) -> p k n", k=k)

        def as_f32(a):
            return a.bitcast(F32)

        GP, GD, GA = {}, {}, {}
        gp = gd = ga = 0
        for name in GDN_STEPS:
            gp += 1
            GP[name] = gp
            ga += {"decay": 3, "norms": 1, "tokens": 1, "kcum": 1, "onorm": 1}.get(name, 1 if name.startswith("lx") else 0)
            GA[name] = ga
            gd += {"scalars": 1, "decay": 1, "norms": 1, "scores": 1, "tokens": 1, "onorm": 2}.get(
                name, 1 if name.startswith(("xlx", "vnew", "state")) else 0)
            GD[name] = gd


        def act_gdn(act, name):
            a = nc.scalar
            if name == "decay":
                act.wait_ge(g_dve, GD["decay"])
                for n in range(2):
                    a.activation(expg[:, H * n:H * n + H, :].rearrange("p a b -> p (a b)"), ps[4 + n][:, :], ACT.Exp)
                a.activation(bexp, gcum, ACT.Exp).then_inc(g_act, 1)
                a.activation(kend_s, kend_s, ACT.Exp).then_inc(g_act, 1)
                a.activation(decayT, decayT, ACT.Exp).then_inc(g_act, 1)
            elif name == "norms":
                act.wait_ge(g_pe, GP["norms"])
                for n in range(4):
                    ins = a.activation(squares[:, 2 * n:2 * n + 2, :].rearrange("p a b -> p (a b)"), ps[4 + n][:, :],
                                       ACT.Sqrt, bias=eps_rms[:, 0:1])
                ins.then_inc(g_act, 1)
            elif name == "tokens":
                act.wait_ge(g_pe, GP["tokens"])
                act.wait_ge(g_act, GA["decay"])
                for p in range(NPB):
                    ins = a.activation(kend[:, p, :], ps[4 + p // 4][:, (p % 4) * P:(p % 4 + 1) * P], ACT.Copy,
                                       scale=kend_s[:, p // H, p % H:p % H + 1])
                ins.then_inc(g_act, 1)
            elif name.startswith("lx"):
                act.wait_ge(g_pe, GP[name])
                for n in range(2):
                    ins = a.copy(T1[:, H * n:H * n + H, :].rearrange("p a b -> p (a b)"), ps[4 + n][:, :])
                ins.then_inc(g_act, 1)
            elif name == "kcum":
                act.wait_ge(g_pe, GP[name])
                for n in range(2):
                    ins = a.mul(nkcT_of(n), ps[4 + n][:, :].rearrange("p (a b) -> p a b", b=P), -1.0)
                ins.then_inc(g_act, 1)
            elif name == "onorm":
                act.wait_ge(g_dve, GD["state3"] + 1)
                a.activation(o_rs, o_ss, ACT.Sqrt, bias=eps_rms[:, 0:1], scale=1.0 / DH).then_inc(g_act, 1)

        def nkcT_of(t):
            return nkcT[:, :, t * P:(t + 1) * P]

        def pt4(h):
            return pT[:, 2 * (h % 2):2 * (h % 2) + 2, :]

        def pe_gdn(pe, name):
            mm, tr = nc.tensor.matmul, nc.tensor.transpose

            def out4(n):
                return ps[4 + n // 4][:, (n % 4) * P:(n % 4 + 1) * P]

            def chunk_T(a, p):
                return a[:, p % H, (p // H) * P:(p // H + 1) * P]

            if name == "scalars":
                pe.wait_ge(g_dve_scal, 1)
                pe.wait_ge(consts, 3)
                mm(ps[3][:, 0:NPB], block_upper[:], g_log, start=True, stop=True)
                ins = mm(ps[3][:, NPB:2 * NPB], block_ones[:], g_log, start=True, stop=True)
            elif name == "decay":
                pe.wait_ge(g_dve, GD["scalars"])
                for p in range(NPB):
                    mm(out4(p), g_rows[:, p, :], block_upper[:], start=True, stop=True)
                for p in range(NPB):
                    ins = mm(out4(NPB + p), beta_rows[:, p, :], ident[:], start=True, stop=True)
            elif name == "norms":
                pe.wait_ge(g_dve_sq, 1)
                pe.wait_ge(g_dve, GD["decay"])
                pe.wait_ge(g_act, GA["decay"])
                for n in range(4):
                    ins = mm(ps[4 + n][:, :], ones[:], squares[:, 2 * n:2 * n + 2, :].rearrange("p a b -> p (a b)"), start=True, stop=True)
            elif name == "scores":
                pe.wait_ge(g_dve, GD["norms"])
                for p in range(NPB):
                    mm(out4(p), chunk_T(kT, p), chunk_T(kT, p), start=True, stop=True)
                for p in range(NPB):
                    ins = mm(out4(NPB + p), chunk_T(kT, p), chunk_T(qT, p), start=True, stop=True)
            elif name == "tokens":
                pe.wait_ge(g_dve, GD["scores"])
                for p in range(NPB):
                    tr(out4(p), chunk_T(kT, p), ident[:])
                for p in range(NPB):
                    ins = tr(out4(NPB + p), chunk_T(vT, p), ident[:])
            elif name.startswith("lx"):
                n = int(name[2:])
                pe.wait_ge(g_pool, n + 1)
                pe.wait_ge(g_dve, GD["tokens"] if n == 0 else GD[f"xlx{n - 1}"])
                pe.wait_ge(g_act, GA["tokens"])
                for p in range(NPB):
                    ins = mm(out4(p), LTs[n % 2][:, p, :], X[:, p, :], start=True, stop=True)
            elif name.startswith("xlx"):
                n = int(name[3:])
                pe.wait_ge(g_act, GA[f"lx{n}"])
                for p in range(NPB):
                    ins = mm(out4(p), T1[:, p, :], XT[:, p, :], start=True, stop=True)
                if n < LEVELS - 1:
                    for p in range(NPB):
                        ins = mm(out4(NPB + p), XT[:, p, :], T1[:, p, :], start=True, stop=True)
            elif name == "kcum":
                pe.wait_ge(g_dve, GD[f"xlx{LEVELS - 1}"])
                for p in range(NPB):
                    ins = mm(out4(p), kbe[:, p, :], XT[:, p, :], start=True, stop=True)
            elif name.startswith("vnew"):
                c = int(name[4:])
                t, lo = c // 2, CHUNK * (c % 2)
                pe.wait_ge(g_act, GA["kcum"])
                if c:
                    pe.wait_ge(g_dve, GD[f"state{c - 1}"])
                for h in range(H):
                    o = ps[6][lo:lo + CHUNK, h * DH:(h + 1) * DH]
                    ins = mm(o, XT[:, t * H + h, lo:lo + CHUNK], vbeta[:, t * H + h, :], start=True, stop=(c == 0))
                    if c:
                        ins = mm(o, nkcT[:, h, t * P + lo:t * P + lo + CHUNK], state[:, h, :], start=False, stop=True)
            elif name.startswith("state"):
                c = int(name[5:])
                t, lo = c // 2, CHUNK * (c % 2)
                pe.wait_ge(g_dve, GD[f"vnew{c}"])
                rows = slice(lo, lo + CHUNK)
                for h in range(H):
                    o = ps[7][rows, h * DH:(h + 1) * DH]
                    if c:
                        mm(o, qT[:, h, t * P + lo:t * P + lo + CHUNK], state[:, h, :], start=True, stop=False)
                    mm(o, decayT[rows, t * H + h, rows], vnew[rows, h, :], start=(c == 0), stop=True)
                for h in range(H):
                    ins = mm(ps[5][:, h * DH:(h + 1) * DH], kend[rows, t * H + h, :], vnew[rows, h, :], start=True, stop=True)
            elif name == "onorm":
                pe.wait_ge(g_dve, GD["onorm"])
                for t in range(NT):
                    for h in range(H):
                        n = h * NT + t
                        ins = tr(out4(n), o_tok[:, t, h * DH:(h + 1) * DH], ident[:])
            ins.then_inc(g_pe, 1)

        def dve_gdn(v, name, step):
            d = nc.vector

            def flat(a):
                return a.rearrange("p a b -> p (a b)")

            if name == "scalars":
                v.wait_ge(g_pe, GP[name])
                step(d.tensor_copy(gcum, ps[3][:, 0:NPB].rearrange("p (t h) -> p t h", t=NT)))
                d.tensor_tensor(kend_s, ps[3][:, NPB:2 * NPB].rearrange("p (t h) -> p t h", t=NT), gcum,
                                ALU.subtract).then_inc(g_dve, 1)
            elif name == "decay":
                v.wait_ge(g_pe, GP[name])
                for p in range(NPB):
                    d.scalar_tensor_tensor(out=decayT[:, p, :], in0=ps[4 + p // 4][:, (p % 4) * P:(p % 4 + 1) * P],
                                           scalar=gcum[:, p // H, p % H:p % H + 1], in1=negmask[:],
                                           op0=ALU.subtract, op1=ALU.add)
                for n in range(2):
                    ins = d.tensor_copy(flat(LT[:, H * n:H * n + H, :]), ps[6 + n][:, :])
                ins.then_inc(g_dve, 1)
            elif name == "norms":
                v.wait_ge(g_act, GA["decay"])
                step(d.tensor_tensor(bexp, bexp, beta, ALU.mult))
                step(d.tensor_copy(chunk_decay, expg[:, :, CHUNK - 1::CHUNK]))
                v.wait_ge(g_act, GA[name])
                step(d.reciprocal(squares, squares))
                d.tensor_tensor(kT, kT, squares[:, H:2 * H, :], ALU.mult)
                d.scalar_tensor_tensor(out=flat(qT), in0=flat(qT), scalar=DH ** -0.5, in1=flat(squares[:, 0:H, :]),
                                       op0=ALU.mult, op1=ALU.mult).then_inc(g_dve, 1)
            elif name == "scores":
                v.wait_ge(g_pe, GP[name])
                step(d.tensor_tensor(LT, LT, decayT, ALU.mult))
                for n in range(2):
                    o = flat(LT[:, H * n:H * n + H, :])
                    step(d.tensor_tensor(o, o, ps[4 + n][:, :], ALU.mult))
                for n in range(2):
                    o = flat(decayT[:, H * n:H * n + H, :])
                    step(d.tensor_tensor(o, o, ps[6 + n][:, :], ALU.mult))
                qv = qT.rearrange("p h (t n) -> p t h n", t=NT)
                ev = expg.rearrange("p (t h) n -> p t h n", t=NT)
                for t in range(NT):
                    ins = d.tensor_tensor(qv[:, t, :, :], qv[:, t, :, :], ev[:, t, :, :], ALU.mult)
                ins.then_inc(g_dve, 1)
            elif name == "tokens":
                for a in (X, XT):
                    step(d.tensor_copy(a, ident[:].rearrange("p (a n) -> p a n", a=1).broadcast_to([P, NPB, P])))
                v.wait_ge(g_pe, GP[name])
                for p in range(NPB):
                    o = ps[6 + p // 4][:, (p % 4) * P:(p % 4 + 1) * P]
                    d.tensor_scalar(vbeta[:, p, :], o, beta[:, p // H, p % H:p % H + 1], None, ALU.mult)
                v.wait_ge(g_act, GA[name])
                for p in range(NPB):
                    o = ps[4 + p // 4][:, (p % 4) * P:(p % 4 + 1) * P]
                    ins = d.tensor_scalar(kbe[:, p, :], o, bexp[:, p // H, p % H:p % H + 1], None, ALU.mult)
                ins.then_inc(g_dve, 1)
            elif name.startswith("xlx"):
                v.wait_ge(g_pe, GP[name])
                last = int(name[3:]) == LEVELS - 1
                for n in range(2):
                    o = flat(XT[:, H * n:H * n + H, :])
                    ins = d.tensor_tensor(o, o, ps[4 + n][:, :], ALU.subtract)
                if not last:
                    for n in range(2):
                        o = flat(X[:, H * n:H * n + H, :])
                        ins = d.tensor_tensor(o, o, ps[6 + n][:, :], ALU.subtract)
                ins.then_inc(g_dve, 1)
            elif name.startswith("vnew"):
                c = int(name[4:])
                rows = slice(CHUNK * (c % 2), CHUNK * (c % 2) + CHUNK)
                v.wait_ge(g_pe, GP[name])
                d.tensor_copy(flat(vnew)[rows, :], ps[6][rows, :]).then_inc(g_dve, 1)
            elif name.startswith("state"):
                c = int(name[5:])
                rows = slice(CHUNK * (c % 2), CHUNK * (c % 2) + CHUNK)
                v.wait_ge(g_pe, GP[name])
                step(d.tensor_copy(o_tok[rows, c // 2, :], ps[7][rows, :]))
                for h in range(H):
                    o = ps[5][:, h * DH:(h + 1) * DH]
                    if c == 0:
                        ins = d.tensor_copy(state[:, h, :], o)
                    else:
                        ins = d.scalar_tensor_tensor(out=state[:, h, :], in0=state[:, h, :],
                                                     scalar=chunk_decay[:, (c // 2) * H + h, c % 2:c % 2 + 1],
                                                     in1=o, op0=ALU.mult, op1=ALU.add)
                ins.then_inc(g_dve, 1)
                v.wait_ge(g_dve, GD[name])
            elif name == "onorm":
                of = o_tok.rearrange("p t (h n) -> p (t h) n", h=H)
                step(d.tensor_tensor(LT, of, of, ALU.mult))
                d.tensor_reduce(o_ss, LT, AX.X, ALU.add).then_inc(g_dve, 1)
                v.wait_ge(g_act, GA[name])
                step(d.reciprocal(o_rs, o_rs))
                d.tensor_tensor(of, of, o_rs.rearrange("p (a b) -> p a b", b=1).broadcast_to([P, NPB, P]),
                                ALU.mult).then_inc(g_dve, 1)
                v.wait_ge(g_pe, GP[name])
                for n in range(2):
                    ins = d.scalar_tensor_tensor(out=flat(yaT)[:, 512 * n:512 * n + 512], in0=ps[4 + n][:, :],
                                                 scalar=small_cols[:, 60:61], in1=flat(zs)[:, 512 * n:512 * n + 512],
                                                 op0=ALU.mult, op1=ALU.mult)
                ins.then_inc(ya_ready, 1)

        def wait_copied(eng, kind, count):
            units = [u for u in UNITS if u[0] == kind][:count]
            for b in range(BANKS):
                turns = [turn_of(u) for u in units if bank_of(u) == b]
                if turns:
                    eng.wait_ge(bank_free[b], max(turns))

        def prep_lo(eng, ops, q, who):
            if lo_engine(q) == who:
                src, hi, lo = piece_views(q)
                eng.wait_ge(split_hi, q + 1)
                ops.tensor_tensor(lo, src, as_f32(hi), ALU.subtract).then_inc(split_lo[who], 1)

        def slot_dma(sp, n):
            kind, c = MIXER_SLOTS[n]
            dst = raw[:, n % RAW, :]
            if kind == "br":
                dst, src = dst.rearrange("p (k n) -> p k n", k=H), w_br[0, c].rearrange("(k p) n -> p k n", p=P)
            else:
                m = {"kv": w_mem_kv, "in": w_in, "wo": w_o}[kind][0]
                dst = dst.rearrange("p (k n) -> p k n", k=KD)
                src = m.rearrange("(k p) n -> p k n", p=P)[:, :, c:c + W]
            if n >= RAW:
                raw_spent(sp, n - RAW)
            sp.dma_start(dst, src).then_inc(raw_in[n % RAW], 16)

        def raw_spent(sp, n):
            for who in split_lo:
                sp.wait_ge(split_lo[who], 2 * (n + 1))

        def chunk_dma(sp, c, gu, dn, dst, landed):
            if c < 4:
                src = gu.rearrange("(k p) n -> p k n", p=P)[:, 2 * c:2 * c + 2, :]
                dst = dst.rearrange("p (k n) -> p k n", k=2)
            else:
                src = dn.rearrange("(k p) n -> p k n", p=P)[:, 4 * (c - 4):4 * (c - 4) + 4, :]
                dst = dst.rearrange("p (k n) -> p k n", k=4)
            sp.dma_start(dst, src).then_inc(landed, 16)

        RING_IN = raw_in + first_in + late_in
        MIXER_FILLS = [len(range(r, N_MIX, RAW)) if r < RAW else 0 for r in range(RING)]

        def ring_place(m, rounds=0):
            r = m % RING
            fill = m // RING + 1 + MIXER_FILLS[r]
            return RING_SLOTS[r], RING_IN[r], (rounds * (ROUND * EC // RING) + fill) * 16

        def item_places(i, rounds=0):
            return [ring_place(EC * i + c, rounds) for c in range(EC)]

        def further_places(i):
            return [(slot, landed, 16 * i + (count - 16 * (NE - 1))) for slot, landed, count in item_places(NE - 1)]

        def chunk_spent(eng, m, items=0):
            i, c = items + m // EC, m % EC
            if c == 3:
                eng.wait_ge(gu_done, i + 1)
            elif c == 5:
                eng.wait_ge(down_done, i + 1)
            else:
                eng.wait_ge(chunks_used, 4 * i + (c + 1 if c < 3 else 4))

        block = ctx.enter_context(nc.Block())

        @block.sync
        def _(sp):
            def bcast(dst, src, done):
                sp.dma_start(dst, src).then_inc(done, 16)

            sp.dma_start(mem_tok, mem[0].rearrange("(t p) d -> p t d", p=P)).then_inc(mem_in, 16)
            slot_dma(sp, 0)
            sp.dma_start(hx[:], x[0].rearrange("(t p) d -> p t d", p=P)).then_inc(x_in, 16)
            bcast(lnp0[:, 0, :], ln0_g.rearrange("(a d) -> a d", a=1).broadcast_to([P, D]), lnp_in[0])
            bcast(lnp0[:, 1, :], ln0_b.rearrange("(a d) -> a d", a=1).broadcast_to([P, D]), lnp_in[0])
            for n in range(1, N_MIX):
                slot_dma(sp, n)
            sp.wait_ge(ya_split, 1)
            sp.wait_ge(yb_split, 1)
            sp.dma_start(bgu[0:NE, :], b_gate_up[0]).then_inc(ebias_in, 16)
            sp.dma_start(bdown[0:NE, :], b_down[0]).then_inc(ebias_in, 16)
            bcast(lnp1[:, 0, :], ln1_g.broadcast_to([P, D]), lnp_in[1])
            bcast(lnp1[:, 1, :], ln1_b.broadcast_to([P, D]), lnp_in[1])
            order = list(range(RAW, EC)) + list(range(RAW))
            for c in order:
                if c < RAW:
                    raw_spent(sp, N_MIX - RAW + (c - N_MIX) % RAW)
                chunk_dma(sp, c, w_gate_up[0, 0], w_down[0, 0], *ring_place(c)[0:2])
            sp.wait_ge(bank_full[bank_of(("wo", 1, 1))], turn_of(("wo", 1, 1)))
            for c in range(EC):
                if EC + c == RING - 1:
                    sp.wait_ge(bank_full[bank_of(("logits", 1))], turn_of(("logits", 1)))
                if EC + c >= RING:
                    chunk_spent(sp, EC + c - RING)
                chunk_dma(sp, c, w_gate_up[0, 1], w_down[0, 1], *ring_place(EC + c)[0:2])
            with sp.Fori(0, ROUNDS) as j:
                for u in range(ROUND):
                    ex = ROUND * j + (2 + u)
                    gu = w_gate_up[0, bass.ds(ex, 1), :, :].rearrange("e d f -> (e d) f")
                    dn = w_down[0, bass.ds(ex, 1), :, :].rearrange("e d f -> (e d) f")
                    for c in range(EC):
                        m = EC * (2 + u) + c
                        chunk_spent(sp, m - RING, ROUND * j)
                        chunk_dma(sp, c, gu, dn, *ring_place(m)[0:2])
            chunk_spent(sp, LAST_IN_LN2_SLOT)
            bcast(lnp2[:, 0, :], ln2_g.broadcast_to([P, D]), lnp_in[2])
            bcast(lnp2[:, 1, :], ln2_b.broadcast_to([P, D]), lnp_in[2])
            sp.wait_ge(r_items, 1)
            n_items = sp.value_load(count_i[0:1, 0:1], min_val=NE, max_val=NE + EXTRA)
            with sp.If_ne(sp.to_reg(n_items), NE):
                with sp.Fori(NE, n_items) as i:
                    ex = sp.value_load(ids_i[0:1, bass.ds(i, 1)], min_val=0, max_val=NE - 1)
                    gu = w_gate_up[0, bass.ds(ex, 1), :, :].rearrange("e d f -> (e d) f")
                    dn = w_down[0, bass.ds(ex, 1), :, :].rearrange("e d f -> (e d) f")
                    for c in range(EC):
                        chunk_spent(sp, c, i - 1)
                        chunk_dma(sp, c, gu, dn, *further_places(i)[c][0:2])
            for t in range(NT):
                sp.wait_ge(ln_done, 2 * NT + t + 1)
                sp.dma_start(out[0, t * P:(t + 1) * P, :], hx[:, t, :]).then_inc(out_stored, 16)
            sp.wait_ge(out_stored, 16 * NT)

        @block.gpsimd
        def _(pool):
            chain = [0]

            def step(ins):
                chain[0] += 1
                ins.then_inc(pool_chain, 1)
                pool.wait_ge(pool_chain, chain[0])

            eng = nc.gpsimd
            step(eng.memset(ones[:], 1.0))
            eng.affine_select(out=ident[:], in_=ones[:], pattern=[[-1, P]], compare_op=ALU.is_equal,
                              fill=0.0, base=0, channel_multiplier=1).then_inc(consts, 1)
            eng.memset(eps_ln, LN_EPS)
            eng.memset(eps_rms, RMS_EPS).then_inc(consts, 1)
            eng.memset(qkv_pad[:, :, 0:3], 0.0)
            eng.memset(upad[:, :, 0:2], 0.0).then_inc(pads, 1)

            def masks():
                eng.affine_select(out=before[:], in_=ones[:], pattern=[[1, P]], compare_op=ALU.is_gt,
                                  fill=0.0, base=0, channel_multiplier=-1)
                for n in range(LEVELS + 1):
                    s = 1 << n
                    v = blocks[:, n, :].rearrange("p (b s) -> p b s", s=s)
                    o = ones[:].rearrange("p (b s) -> p b s", s=s)
                    step(eng.affine_select(out=v, in_=o, pattern=[[-s, P // s], [0, s]],
                                           compare_op=ALU.is_ge, fill=0.0, base=0, channel_multiplier=1))
                    step(eng.affine_select(out=v, in_=v, pattern=[[s, P // s], [0, s]],
                                           compare_op=ALU.is_ge, fill=0.0, base=s - 1, channel_multiplier=-1))
                step(eng.tensor_copy(block_ones[:], blocks[:, LEVELS, :]))
                step(eng.affine_select(out=block_upper[:], in_=block_ones[:], pattern=[[1, P]],
                                       compare_op=ALU.is_ge, fill=0.0, base=0, channel_multiplier=-1))
                step(eng.tensor_scalar(negmask[:], block_upper[:], -1.0, BIG, ALU.add, ALU.mult))
                for n in range(LEVELS):
                    step(eng.tensor_tensor(level_mask[:, n, :], blocks[:, n + 1, :], blocks[:, n, :], ALU.subtract))
                for n in range(LEVELS):
                    ins = eng.affine_select(out=level_mask[:, n, :], in_=level_mask[:, n, :], pattern=[[1, P]],
                                            compare_op=ALU.is_gt, fill=0.0, base=0, channel_multiplier=-1)
                ins.then_inc(consts, 1)

            masks()
            MASK_LEVEL = {("g", "tokens"): 0}
            MASK_LEVEL.update({("g", f"lx{n - 1}"): n for n in range(1, LEVELS)})
            for s in SCHEDULE:
                if s[0] == "prep":
                    prep_lo(pool, eng, s[1], "pool")
                if s in MASK_LEVEL:
                    n = MASK_LEVEL[s]
                    if n == 0:
                        pool.wait_ge(g_dve, GD["scores"])
                    if n >= 2:
                        pool.wait_ge(g_pe, GP[f"lx{n - 2}"])
                    m = level_mask[:, n:n + 1, :].broadcast_to([P, NPB, P])
                    eng.tensor_tensor(LTs[n % 2], LT, m, ALU.mult).then_inc(g_pool, 1)
            pool.wait_ge(sum_split, KD)
            eng.iota(slot_iota.rearrange("p (a b) -> p a b", b=CAP), pattern=[[0, 2], [1, CAP]], base=0,
                     channel_multiplier=0, allow_small_or_imprecise_dtypes=True)
            eng.iota(part_iota, pattern=[[0, P]], base=0, channel_multiplier=1,
                     allow_small_or_imprecise_dtypes=True)
            eng.iota(e_iota, pattern=[[1, NE]], base=0, channel_multiplier=0,
                     allow_small_or_imprecise_dtypes=True)
            eng.memset(ranks, NOT_HERE)
            eng.memset(weights, 0.0)
            eng.memset(ids, 0.0).then_inc(moe_consts, 1)

        @block.scalar
        def _(act):
            chain = [0]
            a = nc.scalar

            def step(ins):
                chain[0] += 1
                ins.then_inc(act_chain, 1)
                act.wait_ge(act_chain, chain[0])

            rows = small_rows
            act.dma_start(rows[0:48, :], conv_qkv[0].rearrange("j (c p) -> (j c) p", p=P)).then_inc(rows_in, 16)
            act.dma_start(rows[48:60, :], conv_mix[0].rearrange("j (c p) -> (j c) p", p=P)).then_inc(rows_in, 16)
            act.dma_start(rows[60:61, :], gdn_norm).then_inc(rows_in, 16)
            act.dma_start(w_ab[:], w_in[0].rearrange("(k p) n -> p k n", p=P)[:, :, C_AB:C_AB + 2 * H]).then_inc(ab_in, 16)
            act.dma_start(adt[:, 0, :], a_log.broadcast_to([P, H])).then_inc(adt_in, 16)
            act.dma_start(adt[:, 1, :], dt_bias.broadcast_to([P, H])).then_inc(adt_in, 16)
            act.dma_start(wr[:], w_router[0].rearrange("(k p) e -> p k e", p=P)).then_inc(router_in, 16)
            act.dma_start(br_bc[:], b_router.broadcast_to([P, NE])).then_inc(router_in, 16)

            def ln_root_of(n, t):
                act.wait_ge(ln_var, NT * n + t + 1)
                a.activation(ln_std[:, t:t + 1], ln_mv[:, t, 1:2], ACT.Sqrt, bias=eps_ln[:, 0:1]).then_inc(ln_root, 1)

            def bank(u, n=T):
                return ps[bank_of(u)][:, 0:n]

            def silu(n):
                act.wait_ge(conv_done, n + 1)
                a.activation(qkvT[:, n, :], qkvT[:, n, :], ACT.Silu).then_inc(silu_done, 1)

            act.wait_ge(consts, 2)
            for s in SCHEDULE:
                kind = s[0]
                if kind in ("memT", "hT", "km", "vm", "z", "xc", "gb", "qm", "gate", "qkv", "pT", "ym", "x1T"):
                    act.wait_ge(bank_full[bank_of(s)], turn_of(s))
                free = bank_free[bank_of(s)] if kind not in NOT_UNITS else None
                if kind == "prep":
                    q = s[1]
                    n = q // 4
                    act.wait_ge(raw_in[n % RAW], 16 * (n // RAW + 1))
                    if q >= SPLITS:
                        act.wait_ge(*piece_end[q - SPLITS])
                        act.wait_ge(split_lo[lo_engine(q - SPLITS)], 2 * ((q - SPLITS) // 4) + (q - SPLITS) % 4 // 2 + 1)
                    src, hi, _ = piece_views(q)
                    a.copy(hi, src).then_inc(split_hi, 1)
                elif kind == "memT":
                    a.copy(src_hi[:, 2 * s[1]:2 * s[1] + 2, :], bank(s, 512).rearrange("p (a b) -> p a b", a=2)).then_inc(bank_hi, 1)
                elif kind == "hT":
                    t, j = s[1:]
                    a.copy(act_hi[:, 4 * j:4 * j + 4, t * P:(t + 1) * P],
                           bank(s, 512).rearrange("p (a b) -> p a b", b=P)).then_inc(bank_hi, 1)
                elif kind == "ln":
                    ln_root_of(*s[1:])
                elif kind == "km":
                    a.copy(kmT[:, s[1], :], bank(s)).then_inc(free, 1)
                elif kind == "vm":
                    a.copy(vm[:, s[1], :], bank(s, 512)).then_inc(free, 1)
                elif kind == "qkv":
                    if s[1] == 0:
                        act.wait_ge(pads, 1)
                    a.copy(qkv_pad[:, s[1], 3:3 + T], bank(s)).then_inc(free, 1)
                    if s[1] >= 1:
                        silu(s[1] - 1)
                    if s[1] == 11:
                        silu(11)
                elif kind == "ab":
                    act.wait_ge(ab_dve, 1)
                    step(a.activation(t_b, t_b, ACT.Exp))
                    step(a.activation(ea, adt[:, 0, :], ACT.Exp))
                    a.activation(t_b, t_b, ACT.Ln, bias=1.0).then_inc(ab_act, 1)
                    a.activation(beta, beta, ACT.Sigmoid).then_inc(ab_act, 1)
                elif kind == "z":
                    a.activation(zs[:, s[1], :], bank(s), ACT.Silu).then_inc(free, 1)
                elif kind == "xc":
                    a.copy(xc[:, s[1], :], bank(s)).then_inc(free, 1)
                elif kind == "gb":
                    a.copy(gb[:, s[1], :], bank(s)).then_inc(free, 1)
                elif kind == "qm":
                    a.copy(qm[:, s[1], :], bank(s)).then_inc(free, 1)
                    if s[1] == 0:
                        act.wait_ge(yb_ready, 1)
                        wait_copied(act, "vm", 2)
                        a.copy(src_hi[:, H:2 * H, :], xc).then_inc(yb_hi, 1)
                elif kind == "score":
                    act.wait_ge(att_max, s[1] + 1)
                    for t in range(NT):
                        ins = a.activation(probs[:, s[1], t, :], ps[bank_of(s)][:, t * T:(t + 1) * T], ACT.Exp,
                                           bias=s_neg[:, s[1], t:t + 1], scale=DH ** -0.5,
                                           accum_out=s_sum[:, s[1], t:t + 1])
                    ins.then_inc(free, 1)
                elif kind == "pT":
                    a.copy(pt4(s[1]).rearrange("p a b -> p (a b)"), bank(s, 512)).then_inc(free, 1)
                elif kind == "ym":
                    a.copy(src_hi[:, s[1], :], bank(s)).then_inc(bank_hi, 1)
                elif kind == "gate":
                    b, c = s[1:]
                    if b == 2:
                        if c == 0:
                            act.wait_ge(yb_split, 1)
                        dst = first_gates[:, c, :]
                    elif b == 1:
                        dst = gates[:, c, :]
                    else:
                        act.wait_ge(gate_used, c + 1)
                        dst = gates[:, c, :]
                    a.activation(dst, bank(s), ACT.Sigmoid).then_inc(free, 1)
                elif kind == "ya":
                    act.wait_ge(ya_ready, 1)
                    act.wait_ge(bank_full[bank_of(("br", 2, KD - 1))], turn_of(("br", 2, KD - 1)))
                    a.copy(src_hi[:, 0:H, :], yaT).then_inc(ya_hi, 1)
                elif kind == "sum":
                    act.wait_ge(sum_ready, s[1] + 1)
                    a.copy(act_hi[:, s[1], :], merged[:, s[1], :]).then_inc(sum_hi, 1)
                elif kind == "x1T":
                    t, j = s[1:]
                    a.copy(x1T[:, 4 * j:4 * j + 4, t * P:(t + 1) * P],
                           bank(s, 512).rearrange("p (a b) -> p a b", b=P)).then_inc(free, 1)
                elif kind == "logits":
                    t = s[1]
                    act.wait_ge(r_max, t + 1)
                    a.activation(el[:, t, :], logits[:, t, :], ACT.Exp, bias=r_neg[:, t:t + 1])
                    a.activation(top_e[:, t, 0:TOPK], top_v[:, t, 0:TOPK], ACT.Exp,
                                 bias=r_neg[:, t:t + 1], accum_out=r_sum[:, t:t + 1]).then_inc(r_exp, 1)
                elif kind == "g":
                    act_gdn(act, s[1])

            def item(i):
                act.wait_ge(gate_cut, i + 1)
                a.activation(sig1, gate1, ACT.Sigmoid, scale=SWIGLU_ALPHA).then_inc(sig_done, 1)
                act.wait_ge(hid_turned, i + 1)
                a.copy(hidT.rearrange("p a b -> p (a b)"), ps[3][:, :]).then_inc(hid_copied, 1)
                act.wait_ge(down_done, i + 1)
                a.copy(y_tok[0:64, :], ps[3][0:64, :]).then_inc(y_copied, 1)

            item(0)
            act.wait_ge(r_items, 1)
            n_items = act.value_load(count_i[0:1, 0:1], min_val=NE, max_val=NE + EXTRA)
            with act.Fori(1, n_items) as i:
                item(i)
            for t in range(NT):
                ln_root_of(2, t)

        @block.tensor
        def _(pe):
            mm = nc.tensor.matmul
            tr = nc.tensor.transpose

            def piece(q):
                n, j = q // 4, q % 4
                pe.wait_ge(split_lo[lo_engine(q)], 2 * n + j // 2 + 1)
                _, hi, lo = piece_views(q)
                return hi, lo

            def three(o, l_hi, l_lo, r_hi, r_lo, start, stop):
                mm(o, l_hi, r_hi, start=start, stop=False)
                mm(o, l_hi, r_lo, start=False, stop=False)
                return mm(o, l_lo, r_hi, start=False, stop=stop)

            def project(s, rhs_hi, rhs_lo, c=0, nk=KD):
                hi, lo = piece(PIECES_OF[s][-1])
                for k in range(nk):
                    ins = three(ps[bank_of(s)][:, 0:T], hi[:, k, c * P:(c + 1) * P], lo[:, k, c * P:(c + 1) * P],
                                rhs_hi[:, k, :], rhs_lo[:, k, :], k == 0, k == nk - 1)
                ins.then_inc(bank_full[bank_of(s)], 1)

            def project_rows(s, lhs_hi, lhs_lo):
                both = [s, s[:-1] + (1,)]
                for j, q in enumerate(PIECES_OF[s]):
                    hi, lo = piece(q)
                    for kk in range(2):
                        k = 2 * j + kk
                        for t, u in enumerate(both):
                            ins = three(ps[bank_of(u)][:, :], lhs_hi[:, k, t * P:(t + 1) * P], lhs_lo[:, k, t * P:(t + 1) * P],
                                        hi[:, kk, :], lo[:, kk, :], k == 0, k == KD - 1)
                            if k == KD - 1:
                                ins.then_inc(bank_full[bank_of(u)], 1)
                    if j < 3:
                        ins.then_inc(joint_piece, 1)

            pe.wait_ge(consts, 1)
            for s in SCHEDULE:
                kind = s[0]
                if kind == "g":
                    pe_gdn(pe, s[1])
                if kind in NOT_UNITS:
                    continue
                b = bank_of(s)
                bk = ps[b]
                for u in ([s, s[:-1] + (1,)] if kind in ("vm", "wo") and s[-1] == 0 else [s]):
                    if unit_at[u] >= BANKS:
                        pe.wait_ge(bank_free[bank_of(u)], turn_of(u) - 1)
                if kind == "memT":
                    if s[1] == 0:
                        pe.wait_ge(mem_in, 16)
                    for k in range(2):
                        for t in range(NT):
                            ins = tr(bk[:, k * T + t * P:k * T + (t + 1) * P],
                                     mem_tok[:, t, (2 * s[1] + k) * P:(2 * s[1] + k + 1) * P], ident[:])
                    ins.then_inc(bank_full[b], 1)
                elif kind == "km":
                    if s[1] == 0:
                        wait_copied(pe, "memT", 4)
                    project(s, src_hi, src_lo)
                elif kind == "vm":
                    if s[1] == 0:
                        project_rows(s, src_hi, src_lo)
                elif kind in ("hT", "x1T"):
                    t, j = s[1:]
                    pe.wait_ge(ln_done, t + 1 if kind == "hT" else NT + t + 1)
                    for k in range(4):
                        ins = tr(bk[:, k * P:(k + 1) * P], hx[:, t, (4 * j + k) * P:(4 * j + k + 1) * P], ident[:])
                    ins.then_inc(bank_full[b], 1)
                elif kind == "ab":
                    pe.wait_ge(rows_in, 48)
                    tr(ps[3][:, 0:61], small_rows[0:61, :], ident[0:61, 0:61]).then_inc(cols_turned, 1)
                    wait_copied(pe, "hT", 4)
                    pe.wait_ge(ab_split, 2)
                    for t in range(NT):
                        for k in range(KD):
                            ins = three(bk[:, t * 2 * H:(t + 1) * 2 * H], act_hi[:, k, t * P:(t + 1) * P],
                                        act_lo[:, k, t * P:(t + 1) * P], w_ab_hi[:, k, :], w_ab_lo[:, k, :],
                                        k == 0, k == KD - 1)
                    ins.then_inc(bank_full[b], 1)
                elif kind in ("qkv", "z", "xc", "gc", "gb", "qm", "gate"):
                    project(s, act_hi, act_lo)
                elif kind == "score":
                    if s[1] == 0:
                        wait_copied(pe, "qm", 4)
                    for t in range(NT):
                        ins = mm(bk[:, t * T:(t + 1) * T], qm[:, s[1], t * P:(t + 1) * P], kmT[:, s[1], :],
                                 start=True, stop=True)
                    ins.then_inc(bank_full[b], 1)
                elif kind == "pT":
                    pe.wait_ge(att_p, s[1] + 1)
                    for m in range(2):
                        for t in range(NT):
                            ins = tr(bk[:, m * T + t * P:m * T + (t + 1) * P], probs[:, s[1], t, m * P:(m + 1) * P], ident[:])
                    ins.then_inc(bank_full[b], 1)
                elif kind == "ym":
                    wait_copied(pe, "pT", s[1] + 1)
                    for m in range(2):
                        ins = mm(bk[:, 0:T], vm[:, m, s[1] * DH:(s[1] + 1) * DH], pt4(s[1])[:, m, :],
                                 start=(m == 0), stop=(m == 1))
                    ins.then_inc(bank_full[b], 1)
                elif kind == "br":
                    if s[2] == 0:
                        if s[1] == 2:
                            wait_copied(pe, "ym", 4)
                        if s[1] == 1:
                            pe.wait_ge(yb_split, 1)
                        if s[1] == 0:
                            pe.wait_ge(ya_split, 1)
                    f = H if s[1] == 1 else 0
                    project(s, src_hi[:, f:f + H, :], src_lo[:, f:f + H, :], c=s[2] % 2, nk=H)
                elif kind == "wo":
                    if s[2] == 0:
                        pe.wait_ge(sum_split, KD)
                        project_rows(s, act_hi, act_lo)
                elif kind == "logits":
                    t = s[1]
                    wait_copied(pe, "x1T", 2 * t + 2)
                    pe.wait_ge(router_in, 32)
                    for k in range(KD):
                        ins = mm(bk[:, 0:NE], x1T[:, k, t * P:(t + 1) * P], wr[:, k, :], start=(k == 0), stop=(k == KD - 1))
                    ins.then_inc(bank_full[b], 1)
                elif kind == "rank":
                    pe.wait_ge(r_mask, 1)
                    mm(bk[:, 0:NE], before[:], mask[:, 0, :], start=True, stop=True)
                    mm(bk[:, NE:2 * NE], ones[:], mask[:, 0, :], start=True, stop=False)
                    mm(bk[:, NE:2 * NE], before[:], mask[:, 1, :], start=False, stop=True)
                    for t in range(NT):
                        ins = mm(bk[0:NE, 2 * NE:2 * NE + 1], mask[:, t, :], ones[:, 0:1], start=(t == 0), stop=(t == 1))
                    ins.then_inc(bank_full[b], 1)

            def gather(first=0, last=KD):
                for k in range(first, last):
                    for t in range(NT):
                        ins = mm(ps[0][:, k * CAP:(k + 1) * CAP], hx[:, t, k * P:(k + 1) * P], onehot[:, t, :],
                                 start=(t == 0), stop=(t == NT - 1))
                if last == KD:
                    ins.then_inc(gathered, 1)

            def gate_up(i, places, amid=True):
                pe.wait_ge(tokens_in, i + 1)
                for bk, at in ((ps[1], 0), (ps[2], FF)):
                    for c in range(2):
                        mm(bk[64 * c:64 * c + 64, :], e_row[0:NE, :], bgu[0:NE, at + 512 * c:at + 512 * (c + 1)],
                           start=True, stop=False)
                for q in range(4):
                    slot, landed, count = places[q]
                    pe.wait_ge(landed, count)
                    w = slot.rearrange("p (k n) -> p k n", k=2)
                    for kk in range(2):
                        k = 2 * q + kk
                        for bk, at in ((ps[1], 0), (ps[2], FF)):
                            for c in range(2):
                                ins = mm(bk[64 * c:64 * c + 64, :], x_slotT[:, k, :],
                                         w[:, kk, at + 512 * c:at + 512 * (c + 1)], start=False, stop=(k == KD - 1))
                    ins.then_inc(chunks_used if q < 3 else gu_done, 1)
                    if amid and q == 0:
                        turn_scatter(i - 1)
                    if amid and q == 1:
                        pe.wait_ge(onehots, i + 2)
                        gather(0, 2)
                    if amid and q == 2:
                        gather(2, 6)

            def turn_hidden(i):
                pe.wait_ge(hid_done, i + 1)
                for c in range(4):
                    ins = tr(ps[3][:, c * P:(c + 1) * P], h_tok[:, c * P:(c + 1) * P], ident[:])
                ins.then_inc(hid_turned, 1)

            def down(i, places):
                pe.wait_ge(hid_copied, i + 1)
                for q in range(2):
                    slot, landed, count = places[4 + q]
                    pe.wait_ge(landed, count)
                    w = slot.rearrange("p (k n) -> p k n", k=4)
                    for kk in range(4):
                        for c in range(2):
                            ins = mm(ps[3][64 * c:64 * c + 64, :], hidT[:, kk, 64 * q:64 * q + 64],
                                     w[:, kk, c * 512:(c + 1) * 512], start=(q == 0 and kk == 0), stop=(q == 1 and kk == 3))
                    ins.then_inc(chunks_used if q < 1 else down_done, 1)

            def turn_scatter(i):
                pe.wait_ge(y_copied, 2 * i + 2)
                for t in range(NT):
                    ins = tr(ps[3][:, t * P:(t + 1) * P], onehot_w[:, t, :], ident[:])
                ins.then_inc(sc_turned, 1)

            def scatter_add(i):
                pe.wait_ge(sc_copied, i + 1)
                for t in range(NT):
                    for c in range(2):
                        ins = mm(ps[4 + 2 * t + c][:, :], scatter[64 * c:64 * c + 64, t * P:(t + 1) * P],
                                 y_tok[64 * c:64 * c + 64, :], start=False, stop=True, skip_group_check=True)
                ins.then_inc(item_done, 1)

            pe.wait_ge(bank_free[bank_of(("rank", 0))], turn_of(("rank", 0)))
            pe.wait_ge(onehots, 1)
            gather()
            pe.wait_ge(ebias_in, 32)
            gate_up(0, item_places(0), amid=False)
            pe.wait_ge(onehots, 2)
            gather()
            for t in range(NT):
                tr(ps[7][0:NE, t * P:(t + 1) * P], ranks[:, t, 0:NE], ident[:])
            for t in range(NT):
                ins = tr(ps[7][0:NE, T + t * P:T + (t + 1) * P], weights[:, t, 0:NE], ident[:])
            ins.then_inc(r_cols, 1)
            turn_hidden(0)
            mm(ps[6][0:NE, 0:1], before[0:NE, 0:NE], ext[0:NE, :], start=True, stop=True)
            mm(ps[6][:, 1:2], ones[0:NE, :], ext[0:NE, :], start=True, stop=True).then_inc(r_cols, 1)
            down(0, item_places(0))
            pe.wait_ge(r_sel, 1)
            for t in range(NT):
                o = ps[6][:, t * EXTRA:(t + 1) * EXTRA]
                mm(o, rankT[0:NE, t * P:(t + 1) * P], sel[0:NE, :], start=True, stop=False)
                mm(o, ones[0:NE, :], selb[0:NE, :], start=False, stop=True)
            for t in range(NT):
                mm(ps[6][:, (2 + t) * EXTRA:(3 + t) * EXTRA], weightT[0:NE, t * P:(t + 1) * P], sel[0:NE, :],
                   start=True, stop=True)
            mm(ps[6][:, 4 * EXTRA:5 * EXTRA], part_iota[0:NE, :], sel[0:NE, :], start=True,
               stop=True).then_inc(r_cols, 1)
            pe.wait_ge(r_items, 1)
            for t in range(NT):
                for c in range(2):
                    mm(ps[4 + 2 * t + c][:, :], weightT[0:NE, t * P:(t + 1) * P], bdown[0:NE, c * 512:(c + 1) * 512],
                       start=True, stop=True, skip_group_check=True)
            n_items = pe.value_load(count_i[0:1, 0:1], min_val=NE, max_val=NE + EXTRA)

            def item(i, places):
                gate_up(i, places)
                scatter_add(i - 1)
                turn_hidden(i)
                gather(6, KD)
                down(i, places)

            with pe.Fori(0, ROUNDS) as j:
                for u in range(ROUND):
                    item(ROUND * j + (1 + u), item_places(1 + u, j))
            with pe.Fori(NE - 1, n_items) as i:
                item(i, further_places(i))
            turn_scatter(n_items - 1)
            scatter_add(n_items - 1)

        @block.vector
        def _(v):
            d = nc.vector
            chain = [0]

            def step(ins):
                chain[0] += 1
                ins.then_inc(dve_chain, 1)
                v.wait_ge(dve_chain, chain[0])

            def half_stats(t, c):
                return d.bn_stats(ln_stats[t][c], hx[:, t, 512 * c:512 * c + 512])

            def layer_norm(n, t, params):
                xt = hx[:, t, :]
                both = tiny.at(12 * t, 12)
                d.bn_aggr(ln_mv[:, t, :], both).then_inc(ln_var, 1)
                v.wait_ge(ln_root, NT * n + t + 1)
                step(d.reciprocal(ln_rstd[:, t:t + 1], ln_std[:, t:t + 1]))
                v.wait_ge(ln_var, NT * n + t + 1)
                step(d.tensor_scalar(xt, xt, ln_mv[:, t, 0:1], ln_rstd[:, t:t + 1], ALU.subtract, ALU.mult))
                step(d.tensor_tensor(xt, xt, params[:, 0, :], ALU.mult))
                d.tensor_tensor(xt, xt, params[:, 1, :], ALU.add).then_inc(ln_done, 1)
                v.wait_ge(ln_done, NT * n + t + 1)

            v.wait_ge(ab_in, 16)
            step(d.tensor_copy(w_ab_hi[:], w_ab[:]))
            d.tensor_tensor(w_ab_lo[:], w_ab[:], as_f32(w_ab_hi[:]), ALU.subtract).then_inc(ab_split, 2)
            hi_parts = 0
            for s in SCHEDULE:
                kind = s[0]
                if kind == "g":
                    dve_gdn(v, s[1], step)
                    continue
                if kind == "prep":
                    prep_lo(v, d, s[1], "dve")
                    continue
                if kind == "ln":
                    n, t = s[1:]
                    if n == 0:
                        if t == 0:
                            v.wait_ge(x_in, 16)
                            v.wait_ge(lnp_in[0], 32)
                        step(half_stats(t, 0))
                        step(half_stats(t, 1))
                        layer_norm(0, t, lnp0)
                    else:
                        if t == 0:
                            v.wait_ge(lnp_in[1], 32)
                        layer_norm(1, t, lnp1)
                    continue
                if kind == "ya":
                    v.wait_ge(ya_hi, 1)
                    d.tensor_tensor(src_lo[:, 0:H, :], yaT, as_f32(src_hi[:, 0:H, :]), ALU.subtract).then_inc(ya_split, 1)
                    continue
                if kind == "sum":
                    c = s[1]
                    v.wait_ge(sum_hi, c + 1)
                    d.tensor_tensor(act_lo[:, c, :], merged[:, c, :], as_f32(act_hi[:, c, :]), ALU.subtract).then_inc(sum_split, 1)
                    continue
                bk = ps[bank_of(s)]
                free = bank_free[bank_of(s)]

                def full():
                    v.wait_ge(bank_full[bank_of(s)], turn_of(s))

                if kind in ("memT", "hT", "ym"):
                    hi_parts += 1
                    v.wait_ge(bank_hi, hi_parts)
                    if kind == "memT":
                        hi, lo = (p[:, 2 * s[1]:2 * s[1] + 2, :] for p in (src_hi, src_lo))
                        src = bk[:, :].rearrange("p (a b) -> p a b", a=2)
                    elif kind == "hT":
                        t, j = s[1:]
                        hi, lo = (p[:, 4 * j:4 * j + 4, t * P:(t + 1) * P] for p in (act_hi, act_lo))
                        src = bk[:, :].rearrange("p (a b) -> p a b", b=P)
                    else:
                        hi, lo = (p[:, s[1], :] for p in (src_hi, src_lo))
                        src = bk[:, 0:T]
                    d.tensor_tensor(lo, src, as_f32(hi), ALU.subtract).then_inc(free, 1)
                elif kind == "qkv":
                    c = s[1]
                    v.wait_ge(bank_free[bank_of(s)], turn_of(s))
                    o = qkvT[:, c, :]
                    step(d.tensor_scalar(o, qkv_pad[:, c, 0:T], small_cols[:, c:c + 1], None, ALU.mult))
                    for j in range(1, 4):
                        ins = d.scalar_tensor_tensor(out=o, in0=qkv_pad[:, c, j:j + T], scalar=small_cols[:, 12 * j + c:12 * j + c + 1],
                                                     in1=o, op0=ALU.mult, op1=ALU.add)
                        if j < 3:
                            step(ins)
                    ins.then_inc(conv_done, 1)
                    if c == 11:
                        v.wait_ge(silu_done, 12)
                        d.tensor_tensor(squares, qkvT[:, 0:2 * H, :], qkvT[:, 0:2 * H, :], ALU.mult).then_inc(g_dve_sq, 1)
                elif kind == "ab":
                    v.wait_ge(cols_turned, 1)
                    d.tensor_copy(small_cols[:, 0:61], ps[3][:, 0:61]).then_inc(cols_ready, 1)
                    v.wait_ge(cols_ready, 1)
                    full()
                    v.wait_ge(adt_in, 32)
                    ab = bk[:, 0:NT * 2 * H].rearrange("p (t n) -> p t n", t=NT)
                    for t in range(NT):
                        step(d.tensor_tensor(pre_g[:, t, :], ab[:, t, 0:H], adt[:, 1, :], ALU.add))
                    d.tensor_copy(beta, ab[:, :, H:2 * H]).then_inc(free, 1)
                    v.wait_ge(free, turn_of(s))
                    step(d.tensor_scalar(t_a, pre_g, -1.0, None, ALU.mult))
                    d.tensor_tensor(t_b, t_a, pre_g, ALU.min).then_inc(ab_dve, 1)
                    step(d.tensor_scalar(t_c, pre_g, 0.0, None, ALU.max))
                elif kind == "vm" and s[1] == 1:
                    v.wait_ge(ab_act, 2)
                    step(d.tensor_tensor(t_c, t_c, t_b, ALU.add))
                    for t in range(NT):
                        step(d.scalar_tensor_tensor(out=g_log[:, t, :], in0=t_c[:, t, :], scalar=-1.0, in1=ea,
                                                    op0=ALU.mult, op1=ALU.mult))
                    d.tensor_copy(g_rows.rearrange("p (t h) n -> p t h n", t=NT),
                                  g_log.rearrange("p t (h a) -> p t h a", a=1).broadcast_to([P, NT, H, P]))
                    d.tensor_copy(beta_rows.rearrange("p (t h) n -> p t h n", t=NT),
                                  beta.rearrange("p t (h a) -> p t h a", a=1).broadcast_to([P, NT, H, P])).then_inc(g_dve_scal, 1)
                elif kind == "gc":
                    full()
                    if s[1] == 0:
                        wait_copied(v, "xc", 4)
                        v.wait_ge(pads, 1)
                    d.tensor_tensor(upad[:, s[1], 2:2 + T], bk[:, 0:T], xc[:, s[1], :], ALU.mult).then_inc(free, 1)
                elif kind == "gb":
                    c = s[1]
                    if c == 0:
                        wait_copied(v, "gc", 4)
                    o = xc[:, c, :]
                    step(d.tensor_scalar(o, upad[:, c, 0:T], small_cols[:, 48 + c:49 + c], None, ALU.mult))
                    for j in range(1, 3):
                        step(d.scalar_tensor_tensor(out=o, in0=upad[:, c, j:j + T], scalar=small_cols[:, 48 + 4 * j + c:49 + 4 * j + c],
                                                    in1=o, op0=ALU.mult, op1=ALU.add))
                    v.wait_ge(bank_free[bank_of(s)], turn_of(s))
                    ins = d.tensor_tensor(o, o, gb[:, c, :], ALU.mult)
                    if c == 3:
                        ins.then_inc(yb_ready, 1)
                elif kind == "qm" and s[1] == 1:
                    v.wait_ge(yb_hi, 1)
                    d.tensor_tensor(src_lo[:, H:2 * H, :], xc, as_f32(src_hi[:, H:2 * H, :]), ALU.subtract).then_inc(yb_split, 1)
                elif kind == "score":
                    full()
                    h = s[1]
                    step(d.tensor_reduce(s_max[:, h, :], bk[:, :].rearrange("p (t m) -> p t m", t=NT), AX.X, ALU.max))
                    d.tensor_scalar(s_neg[:, h, :], s_max[:, h, :], -DH ** -0.5, None, ALU.mult).then_inc(att_max, 1)
                elif kind == "pT":
                    h = s[1]
                    v.wait_ge(bank_free[bank_of(("score", h))], turn_of(("score", h)))
                    step(d.reciprocal(s_rec[:, h, :], s_sum[:, h, :]))
                    for t in range(NT):
                        ins = d.tensor_scalar(probs[:, h, t, :], probs[:, h, t, :], s_rec[:, h, t:t + 1], None, ALU.mult)
                    ins.then_inc(att_p, 1)
                elif kind == "br":
                    full()
                    b, c = s[1], s[2]
                    v.wait_ge(bank_free[bank_of(("gate", b, c))], turn_of(("gate", b, c)))
                    m = merged[:, c, :]
                    if b == 2:
                        d.tensor_tensor(m, bk[:, 0:T], first_gates[:, c, :], ALU.mult).then_inc(free, 1)
                    else:
                        gt = gates[:, c, :]
                        d.tensor_tensor(gt, bk[:, 0:T], gt, ALU.mult).then_inc(free, 1)
                        v.wait_ge(free, turn_of(s))
                        d.tensor_tensor(m, m, gt, ALU.add).then_inc(gate_used if b == 1 else sum_ready, 1)
                elif kind == "wo":
                    full()
                    n, t = s[1:]
                    o = hx[:, t, 512 * n:512 * n + 512]
                    d.scalar_tensor_tensor(out=o, in0=o, scalar=ALPHA, in1=bk[:, :], op0=ALU.mult, op1=ALU.add).then_inc(free, 1)
                    v.wait_ge(free, turn_of(s))
                    step(half_stats(t, n))
                elif kind == "logits":
                    t = s[1]
                    if t == 0:
                        v.wait_ge(router_in, 32)
                        v.wait_ge(moe_consts, 1)
                    full()
                    d.tensor_tensor(logits[:, t, :], bk[:, 0:NE], br_bc[:], ALU.add).then_inc(free, 1)
                    v.wait_ge(free, turn_of(s))
                    step(d.max(top_v[:, t, :], logits[:, t, :]))
                    step(d.max_index(top_i[:, t, :], top_v[:, t, :], logits[:, t, :]))
                    d.tensor_scalar(r_neg[:, t:t + 1], top_v[:, t, 0:1], -1.0, None, ALU.mult).then_inc(r_max, 1)
                    step(d.tensor_copy(top_f[:, t, :], top_i[:, t, :]))
                    step(d.tensor_scalar(mask[:, t, :], e_iota, top_f[:, t, 0:1], None, ALU.is_equal))
                    for k in range(1, TOPK):
                        ins = d.scalar_tensor_tensor(out=mask[:, t, :], in0=e_iota, scalar=top_f[:, t, k:k + 1],
                                                     in1=mask[:, t, :], op0=ALU.is_equal, op1=ALU.add)
                        if k < TOPK - 1 or t == 0:
                            step(ins)
                    if t == 1:
                        ins.then_inc(r_mask, 1)
                        v.wait_ge(r_mask, 1)
                        v.wait_ge(r_exp, 2)
                        step(d.reciprocal(r_rec, r_sum))
                        for u in range(NT):
                            step(d.scalar_tensor_tensor(out=weights[:, u, 0:NE], in0=el[:, u, :], scalar=r_rec[:, u:u + 1],
                                                        in1=mask[:, u, :], op0=ALU.mult, op1=ALU.mult))
                        step(d.tensor_copy(ids[:, 0:NE], e_iota))
                elif kind == "rank":
                    full()
                    for t in range(NT):
                        step(d.scalar_tensor_tensor(out=ranks[:, t, 0:NE], in0=mask[:, t, :], scalar=-NOT_HERE,
                                                    in1=bk[:, t * NE:(t + 1) * NE], op0=ALU.mult, op1=ALU.add))
                    step(d.tensor_scalar(ranks[:, :, 0:NE], ranks[:, :, 0:NE], NOT_HERE, None, ALU.add))
                    d.tensor_copy(cnt[0:NE, :], bk[0:NE, 2 * NE:2 * NE + 1]).then_inc(free, 1)
                    v.wait_ge(free, turn_of(s))

            def expert_row(i):
                return d.tensor_scalar(e_row[0:NE, :], part_iota[0:NE, 0:CAP], ids[0:NE, bass.ds(i, 1)], None, ALU.is_equal)

            def one_hots(i):
                for t in range(NT):
                    ins = d.tensor_scalar(onehot[:, t, :], slot_iota[:, 0:CAP], ranks[:, t, bass.ds(i, 1)], None, ALU.is_equal)
                ins.then_inc(onehots, 1)

            def weighted_one_hots(i):
                for t in range(NT):
                    d.tensor_scalar(onehot_w[:, t, :], slot_iota, ranks[:, t, bass.ds(i, 1)],
                                    weights[:, t, bass.ds(i, 1)], ALU.is_equal, ALU.mult)

            def copy_tokens():
                d.tensor_copy(x_slotT.rearrange("p a b -> p (a b)"), ps[0][:, :]).then_inc(tokens_in, 1)

            def hidden(i):
                v.wait_ge(gu_done, i + 1)
                d.tensor_scalar(gate1, ps[1][:, :], LIMIT, None, ALU.min).then_inc(gate_cut, 1)
                d.tensor_scalar(up1, ps[2][:, :], LIMIT, -LIMIT, ALU.min, ALU.max).then_inc(up_cut, 1)
                v.wait_ge(up_cut, i + 1)
                v.wait_ge(gate_cut, i + 1)
                d.scalar_tensor_tensor(out=up1, in0=up1, scalar=1.0, in1=gate1, op0=ALU.add, op1=ALU.mult).then_inc(up_gate, 1)
                v.wait_ge(up_gate, i + 1)
                v.wait_ge(sig_done, i + 1)
                d.tensor_tensor(h_tok, up1, sig1, ALU.mult).then_inc(hid_done, 1)

            def copy_y(i):
                v.wait_ge(down_done, i + 1)
                d.tensor_copy(y_tok[64:128, :], ps[3][64:128, :]).then_inc(y_copied, 1)

            def copy_scatter(i):
                v.wait_ge(sc_turned, i + 1)
                d.tensor_copy(scatter, ps[3][:, 0:T]).then_inc(sc_copied, 1)

            one_hots(0)
            expert_row(0)
            v.wait_ge(gathered, 1)
            copy_tokens()
            step(d.tensor_scalar(ext[0:NE, :], cnt[0:NE, :], float(CAP), None, ALU.is_gt))
            for b in (2, 3):
                step(d.tensor_scalar(ext2[0:NE, :], cnt[0:NE, :], float(CAP * b), None, ALU.is_gt))
                step(d.tensor_tensor(ext[0:NE, :], ext[0:NE, :], ext2[0:NE, :], ALU.add))
            one_hots(1)
            weighted_one_hots(0)
            hidden(0)
            expert_row(1)
            v.wait_ge(gathered, 2)
            copy_tokens()
            v.wait_ge(r_cols, 2)
            step(d.tensor_copy(rankT[0:NE, :], ps[7][0:NE, 0:T]))
            step(d.tensor_copy(weightT[0:NE, :], ps[7][0:NE, T:2 * T]))
            step(d.tensor_scalar(q16[0:NE, :], e_iota[0:NE, 0:EXTRA], ps[6][0:NE, 0:1], None, ALU.subtract))
            step(d.tensor_scalar(sel[0:NE, :], q16[0:NE, :], ext[0:NE, :], None, ALU.is_lt))
            step(d.scalar_tensor_tensor(out=sel[0:NE, :], in0=q16[0:NE, :], scalar=0.0, in1=sel[0:NE, :],
                                        op0=ALU.is_ge, op1=ALU.mult))
            step(d.tensor_scalar(q16[0:NE, :], q16[0:NE, :], 1.0, -float(CAP), ALU.add, ALU.mult))
            step(d.tensor_tensor(selb[0:NE, :], q16[0:NE, :], sel[0:NE, :], ALU.mult))
            d.tensor_scalar(count_i[0:1, :], ps[6][0:1, 1:2], float(NE), None, ALU.add).then_inc(r_sel, 1)
            v.wait_ge(r_cols, 3)
            step(d.tensor_copy(ranks[:, :, NE:NE + EXTRA], ps[6][:, 0:2 * EXTRA].rearrange("p (t n) -> p t n", t=NT)))
            step(d.tensor_copy(weights[:, :, NE:NE + EXTRA], ps[6][:, 2 * EXTRA:4 * EXTRA].rearrange("p (t n) -> p t n", t=NT)))
            step(d.tensor_copy(ids[:, NE:NE + EXTRA], ps[6][:, 4 * EXTRA:5 * EXTRA]))
            d.tensor_copy(ids_i[0:1, :], ids[0:1, :]).then_inc(r_items, 1)
            v.wait_ge(r_items, 1)
            copy_y(0)
            n_items = v.value_load(count_i[0:1, 0:1], min_val=NE, max_val=NE + EXTRA)
            with v.Fori(1, n_items) as i:
                one_hots(i + 1)
                copy_scatter(i - 1)
                weighted_one_hots(i)
                hidden(i)
                expert_row(i + 1)
                v.wait_ge(gathered, i + 2)
                copy_tokens()
                copy_y(i)
            copy_scatter(n_items - 1)
            v.wait_ge(item_done, n_items)
            v.wait_ge(lnp_in[2], 32)
            for t in range(NT):
                for c in range(2):
                    o = hx[:, t, 512 * c:512 * c + 512]
                    step(d.scalar_tensor_tensor(out=o, in0=o, scalar=ALPHA, in1=ps[4 + 2 * t + c][:, :], op0=ALU.mult, op1=ALU.add))
                    step(half_stats(t, c))
                layer_norm(2, t, lnp2)


_INS = ['x', 'mem', 'ln0_g', 'ln0_b', 'w_in', 'conv_qkv', 'conv_mix', 'a_log', 'dt_bias', 'gdn_norm',
        'w_mem_kv', 'w_br', 'w_o', 'ln1_g', 'ln1_b', 'w_router', 'b_router', 'w_gate_up', 'b_gate_up',
        'w_down', 'b_down', 'ln2_g', 'ln2_b']
_OUTS = [((1, T, D), 'float32')]


def kernel(**inputs):
    import numpy as _np
    import concourse.bacc as _bacc
    from concourse import mybir as _mybir
    from concourse.bass_utils import run_bass_kernel_spmd as _run

    nc = _bacc.Bacc("TRN2", target_bir_lowering=False, num_devices=1)
    arrays, args = {}, []
    for name in _INS:
        a = _np.ascontiguousarray(inputs[name])
        arrays[f"in_{name}_dram"] = a
        args.append(nc.dram_tensor(f"in_{name}_dram", a.shape, _mybir.dt.from_np(a.dtype), kind="ExternalInput").ap())
    for i, (shape, dtype) in enumerate(_OUTS):
        dt = _mybir.dt.from_np(_np.dtype(dtype))
        args.append(nc.dram_tensor(f"out_{i}_dram", shape, dt, kind="ExternalOutput").ap())
    hybrid_layer(nc, *args)
    r = _run(nc, [arrays], core_ids=[0])
    return r.results[0]["out_0_dram"]
```

```python
from contextlib import ExitStack

import concourse.bass as bass
from concourse import mybir

F32 = mybir.dt.float32
F32R = mybir.dt.float32r
I32 = mybir.dt.int32
U32 = mybir.dt.uint32
BF16 = mybir.dt.bfloat16
ALU = mybir.AluOpType
ACT = mybir.ActivationFunctionType
AX = mybir.AxisListType

P = 128
D = 1024
T = 256
NT = T // P
KD = D // P
H = 4
DH = 128
W = H * DH
NMEM = 256
CHUNK = 64
NPB = NT * H
LEVELS = 6
NE = 32
TOPK = 4
FF = 1024
CAP = 64
EXTRA = T * TOPK // CAP
ITEMS = NE + EXTRA + 1
SLOT = 4096
RAW = 3
PIECE = SLOT // 4
SPLITS = 3
EC = 6
RING = 10
ROUND = 5
ROUNDS = (NE - 2) // ROUND
assert ROUND * EC % RING == 0 and ROUNDS * ROUND == NE - 2
LN_EPS = 1e-5
RMS_EPS = 1e-6
ALPHA = 2 ** 0.25
LIMIT = 7.0
SWIGLU_ALPHA = 1.702
NOT_HERE = 1000.0
BIG = 1e30

C_QKV, C_AB = 0, 3 * W
C_Z = C_AB + 2 * H
C_XC, C_GB, C_GC, C_QM = C_Z + W, C_Z + 2 * W, C_Z + 3 * W, C_Z + 4 * W
C_GL = C_Z + 5 * W

MIXER_SLOTS = (
    [("kv", 0), ("kv", W)]
    + [("in", C_QKV + W * n) for n in range(3)]
    + [("in", c) for c in (C_Z, C_XC, C_GC, C_GB, C_QM)]
    + [s for b in (2, 1, 0) for s in (("in", C_GL + D * b), ("in", C_GL + D * b + W), ("br", b))]
    + [("wo", 0), ("wo", W)]
)
N_MIX = len(MIXER_SLOTS)

GDN_STEPS = (
    ["scalars", "decay", "norms", "lengths", "scores", "tokens"]
    + ["lx0"] + [f"{half}{n}" for n in range(1, LEVELS) for half in ("lx", "xlx")]
    + ["kcum"]
    + [f"{half}{n}" for n in range(T // CHUNK) for half in ("vnew", "state")]
    + ["olen", "onorm"]
)


def mixer_schedule():
    order = [("memT", n) for n in range(3)] + [("prep", 0), ("memT", 3), ("prep", 1), ("prep", 2), ("ln", 0, 0)]
    order += [("km", 0), ("ln", 0, 1), ("km", 1), ("km", 2), ("km", 3)]
    order += [("hT", t, j) for t in range(NT) for j in range(2)] + [("ab", 0), ("abT", 0), ("log decay",)]
    order += [("vm", n) for n in range(NT)]
    order += [("g", "scalars"), ("qkv", 0), ("qkv", 1), ("g", "decay"), ("qkv", 2)]
    order += [("qkv", n) for n in range(3, 12)]
    g = [s for s in GDN_STEPS if s not in ("scalars", "decay", "olen", "onorm")]
    long = [(kind, n) for kind in ("z", "xc", "gc", "gb", "qm") for n in range(4)]
    order += [long.pop(0) for _ in range(2)]
    for unit in long:
        order += [unit]
        if unit not in (("xc", 0), ("xc", 2)):
            order += [("g", g.pop(0))]
        if unit[0] == "qm":
            order += [("score", unit[1])] + ([("soft", unit[1] - 1)] if unit[1] else [])
    order += [("soft", H - 1)]
    attention = [("pT", 0), ("pT", 1), ("ym", 0), ("pT", 2), ("ym", 1), ("pT", 3), ("ym", 2), ("ym", 3)]
    for n in range(KD):
        order += [("gate", 2, n)]
        order += [attention.pop(0)]
        order += [("g", s) for s in g[:2 if len(g) > KD - n else 1]]
        g = g[2 if len(g) > KD - n else 1:]
    assert not g and not attention
    for b in (2, 1, 0):
        order += [("gate", b, n) for n in range(KD)] if b < 2 else []
        for n in range(KD):
            order += [("br", b, n)]
            if b == 0:
                order += [("sum hi", n)] + ([("sum", n - 1)] if n else [])
            if b == 2:
                order += {0: [("g", "olen")], 3: [("g", "onorm")]}.get(n, [])
        order += [("sum", KD - 1)] if b == 0 else []
        order += [("ya", 0)] if b == 2 else []
    for n in range(2):
        order += [("wo", n, t) for t in range(NT)]
    order += [("ln", 1, t) for t in range(NT)]
    for t in range(NT):
        order += [("x1T", t, j) for j in range(2)] + [("logits", t)]
    order += [("rank", 0)]
    assert SPLITS == 3
    out, q = [], 0
    uses = {}
    for s in order:
        n = {"km": 1, "qkv": 1, "z": 1, "xc": 1, "gc": 1, "gb": 1, "qm": 1, "gate": 1}.get(s[0], 0)
        if s[0] == "br":
            n = s[2] % 2
            uses[s] = [q]
        if s[0] in ("vm", "wo"):
            n = 4 * (s[-1] == 0)
        if n:
            uses[s] = list(range(q, q + n))
            out += [("prep", m + SPLITS) for m in uses[s] if m + SPLITS < 4 * N_MIX]
            q += n
        out.append(s)
    assert q == 4 * N_MIX
    return out, uses


SCHEDULE, PIECES_OF = mixer_schedule()
NOT_UNITS = ("g", "prep", "ln", "ya", "sum hi", "sum", "soft", "log decay")
UNITS = [s for s in SCHEDULE if s[0] not in NOT_UNITS]
BANKS = 3


def hybrid_layer(nc, x, mem, ln0_g, ln0_b, w_in, conv_qkv, conv_mix, a_log, dt_bias, gdn_norm,
                 w_mem_kv, w_br, w_o, ln1_g, ln1_b, w_router, b_router, w_gate_up, b_gate_up,
                 w_down, b_down, ln2_g, ln2_b, out):
    with ExitStack() as ctx:
        def sb(name, shape, dt=F32, scope=ctx):
            return scope.enter_context(nc.sbuf_tensor(name, shape, dt))

        def sem(name):
            return ctx.enter_context(nc.semaphore(name))

        ROW_MIX, ROW_NORM, ROW_G, ROW_B, N_ROWS = 48, 60, 61, 61 + KD, 61 + 2 * KD

        ps = [ctx.enter_context(nc.psum_tensor(f"bank{n}", [P, 512], F32)) for n in range(8)]

        class Space:

            def __init__(self, tensor, size):
                self.tensor, self.size, self.used = tensor, size, 0

            def at(self, start, *shape):
                n = 1
                for k in shape:
                    n *= k
                assert start + n <= self.size, (start + n, self.size)
                a = self.tensor[:, start:start + n]
                if len(shape) == 2:
                    a = a.rearrange("p (a b) -> p a b", b=shape[1])
                return a

            def new(self, *shape):
                a, n = self.at(self.used, *shape), 1
                for k in shape:
                    n *= k
                self.used += n
                return a

        hx = sb("hx", [P, NT, D])
        raw = sb("raw", [P, RAW, SLOT])
        wr = sb("wr", [P, KD, NE])
        br_bc = sb("br_bc", [P, NE])
        ident = sb("ident", [P, P])
        ones = sb("ones", [P, P])
        block_upper = sb("block_upper", [P, P])
        block_ones = sb("block_ones", [P, P])
        negmask = sb("negmask", [P, P])
        alpha_ident = sb("alpha_ident", [P, P])
        before = sb("before", [P, P])
        level_mask = sb("level_mask", [P, LEVELS, P], BF16)
        small_rows = sb("small_rows", [N_ROWS, P])
        small_cols = sb("small_cols", [P, N_ROWS])
        w_ab_hi = sb("w_ab_hi", [P, KD, 2 * H], F32R)
        w_ab_lo = sb("w_ab_lo", [P, KD, 2 * H], F32R)
        adt = sb("adt", [P, 2, H])
        top_i = sb("top_i", [P, NT, 8], U32)
        ids_i = sb("ids_i", [1, ITEMS], I32)
        count_i = sb("count_i", [1, 1], I32)
        tiny = Space(sb("tiny", [P, 204]), 204)
        ln_stats = [[tiny.new(6) for _ in range(2)] for _ in range(NT)]
        ln_mv, ln_std, ln_rstd = tiny.new(NT, 2), tiny.new(NT), tiny.new(NT)
        eps_ln, eps_rms = tiny.new(1), tiny.new(1)
        pre_g, beta = tiny.new(NT, H), tiny.new(NT, H)
        t_a, t_b, t_c = tiny.new(NT, H), tiny.new(NT, H), tiny.new(NT, H)
        g_log, ea = tiny.new(NT, H), tiny.new(H)
        gcum, bexp, kend_s = tiny.new(NT, H), tiny.new(NT, H), tiny.new(NT, H)
        chunk_decay = tiny.new(NPB, 2)
        s_max, s_neg, s_sum, s_rec = (tiny.new(H, NT) for _ in range(4))
        o_ss, o_rs = tiny.new(NPB), tiny.new(NPB)
        inv_norm = tiny.new(NT, 2 * H)

        early = ExitStack()
        EARLY = 22000
        e = Space(sb("early", [P, EARLY], scope=early), EARLY)
        R = 1024
        o_pad = e.used; qkv_pad = e.new(12, T + 3)
        squares = e.at(o_pad, 2 * H, T)
        T1, LTs = e.at(o_pad, NPB, P), [e.at(o_pad + R, NPB, P), e.at(o_pad + 2 * R, NPB, P)]
        nkcT, o_tok = e.at(o_pad, H, T), e.at(o_pad + R, NT, W)
        o_qkv = e.used; qkvT = e.new(12, T)
        blocks = e.at(o_qkv, LEVELS + 1, P)
        qT, kT, vT = qkvT[:, 0:H, :], qkvT[:, H:2 * H, :], qkvT[:, 2 * H:3 * H, :]
        kbe, vbeta = e.at(o_qkv + R, NPB, P), e.at(o_qkv + 2 * R, NPB, P)
        decayT_o = e.used; decayT = e.new(NPB, P)
        yaT = e.at(decayT_o, H, T)
        o_eb = e.used; expg = e.new(NPB, P)
        state, vnew = e.at(o_eb, H, DH), e.at(o_eb + W, H, DH)
        LT = e.new(NPB, P)
        kend = e.new(NPB, P)
        o_gb = e.used + H * T
        zs, gb, xc, qm = (e.new(H, T) for _ in range(4))
        first_gates = e.at(o_gb, KD, T)
        kmT, vm = e.new(H, NMEM), e.new(NT, W)
        upad_o = e.used; upad = e.new(H, T + 2)
        pT = e.at(upad_o, H, T)
        DEAD = e.used
        o_x = e.used; X, XT = e.new(NPB, P), e.new(NPB, P)
        lnp0 = e.at(o_x, 2, D)
        merged = e.at(o_x, KD, T)
        o_mem = e.used; mem_tok = e.new(NT, D)
        probs = e.at(o_mem, H, 2 * T).rearrange("p h (t m) -> p h t m", t=NT)
        gates = e.at(o_mem, KD, T)
        GATED = e.used
        act_hi, act_lo = (sb(n, [P, KD, T], F32R, early) for n in ("act_hi", "act_lo"))
        src_hi, src_lo = (sb(n, [P, KD, T], F32R, early) for n in ("src_hi", "src_lo"))
        w_ab = e.at(o_qkv + R, KD, 2 * H)
        ab_rows = e.at(o_qkv, T)                 
        w_hi, w_lo = (sb(n, [P, SPLITS, PIECE], F32R, early) for n in ("w_hi", "w_lo"))
        early.close()

        LATE = 36610
        l = Space(sb("late", [P, LATE]), LATE)
        first_slots = [l.new(SLOT) for _ in range(3)]
        bgu, bdown = l.new(2 * FF), l.new(D)
        lnp1 = l.new(2, D)
        assert l.used <= DEAD
        x_slotT = l.new(KD, CAP)
        up1, gate1 = l.new(512), l.new(512)
        h_tok = gate1
        slot_iota, part_iota, e_iota = l.new(P), l.new(P), l.new(NE)
        e_row = l.new(CAP)
        onehot, onehot_w = l.new(NT, CAP), l.new(NT, P)
        ranks, weights, ids = l.new(NT, ITEMS), l.new(NT, ITEMS), l.new(ITEMS)
        logits, el, mask = l.new(NT, NE), l.new(NT, NE), l.new(NT, NE)
        top_v, top_f, top_e = l.new(NT, 8), l.new(NT, 8), l.new(NT, 8)
        r_neg, r_sum, r_rec = l.new(NT), l.new(NT), l.new(NT)
        q16, sel, selb = l.new(EXTRA), l.new(EXTRA), l.new(EXTRA)
        cnt, ext, ext2 = l.new(1), l.new(1), l.new(1)
        assert l.used <= GATED, (l.used, GATED)
        hidT = lnp1[:, 0, 0:512].rearrange("p (a b) -> p a b", b=P)
        y_tok = lnp1[:, 0, 512:1024]
        scatter = lnp1[:, 1, 0:T]
        weightT = lnp1[:, 1, T:2 * T]
        sig1 = lnp1[:, 1, 512:1024]
        rankT = sig1[:, 0:T]
        late_slots = [l.new(SLOT) for _ in range(4)]
        x1T = l.at(l.used - KD * T, KD, T)

        RING_SLOTS = [raw[:, n, :] for n in range(RAW)] + first_slots + late_slots
        assert len(RING_SLOTS) == RING
        LN2_SLOT = RAW
        LAST_IN_LN2_SLOT = max(m for m in range(NE * EC) if m % RING == LN2_SLOT)
        assert LAST_IN_LN2_SLOT < (NE - 1) * EC
        lnp2 = RING_SLOTS[LN2_SLOT][:, 0:2 * D].rearrange("p (a b) -> p a b", a=2)

        x_in, mem_in = sem("x_in"), sem("mem_in")
        rows_in, ab_in, adt_in = sem("rows_in"), sem("ab_in"), sem("adt_in")
        lnp_in = [sem(f"lnp{n}_in") for n in range(3)]
        router_in, ebias_in = sem("router_in"), sem("ebias_in")
        piece_in = [sem(f"piece_in{n}") for n in range(4)]
        raw_in = [sem(f"raw_in{n}") for n in range(RAW)]
        first_in = [sem(f"first_in{n}") for n in range(3)]
        late_in = [sem(f"late_in{n}") for n in range(4)]
        split_hi = sem("split_hi")
        split_lo = {"dve": sem("split_lo_dve"), "pool": sem("split_lo_pool")}
        joint_piece = sem("joint_piece")
        bank_full = [sem(f"bank_full{n}") for n in range(BANKS)]
        bank_free = [sem(f"bank_free{n}") for n in range(BANKS)]
        bank_hi = sem("bank_hi")
        x1_ready = sem("x1_ready")
        consts, pads = sem("consts"), sem("pads")
        cols_turned, cols_ready = sem("cols_turned"), sem("cols_ready")
        pool_chain, dve_chain, act_chain = sem("pool_chain"), sem("dve_chain"), sem("act_chain")
        ln_var, ln_root, ln_done = sem("ln_var"), sem("ln_root"), sem("ln_done")
        conv_done, silu_done = sem("conv_done"), sem("silu_done")
        g_pe, g_dve, g_act, g_pool = sem("g_pe"), sem("g_dve"), sem("g_act"), sem("g_pool")
        ab_split, ab_act, ab_dve = sem("ab_split"), sem("ab_act"), sem("ab_dve")
        g_dve_scal, g_dve_sq = sem("g_dve_scal"), sem("g_dve_sq")
        att_max, att_p = sem("att_max"), sem("att_p")
        gate_used = sem("gate_used")
        yb_ready, yb_hi, yb_split = sem("yb_ready"), sem("yb_hi"), sem("yb_split")
        ya_ready, ya_hi, ya_split = sem("ya_ready"), sem("ya_hi"), sem("ya_split")
        sum_ready, sum_hi, sum_split = sem("sum_ready"), sem("sum_hi"), sem("sum_split")
        r_max, r_exp, r_mask, r_ext, r_counted, r_sel, r_cols, r_items = (sem(n) for n in (
            "r_max", "r_exp", "r_mask", "r_ext", "r_counted", "r_sel", "r_cols", "r_items"))
        moe_consts = sem("moe_consts")
        onehots, gathered, tokens_in = sem("onehots"), sem("gathered"), sem("tokens_in")
        chunks_used = sem("chunks_used")
        gu_done, gate_cut, sig_done, hid_done = sem("gu_done"), sem("gate_cut"), sem("sig_done"), sem("hid_done")
        up_cut, up_gate = sem("up_cut"), sem("up_gate")
        hid_turned, hid_copied = sem("hid_turned"), sem("hid_copied")
        down_done, y_copied = sem("down_done"), sem("y_copied")
        sc_turned, sc_copied, tile_done = sem("sc_turned"), sem("sc_copied"), sem("tile_done")
        half_out, out_stored = sem("half_out"), sem("out_stored")

        unit_at = {u: n for n, u in enumerate(UNITS)}

        def bank_of(u):
            return unit_at[u] % BANKS

        def turn_of(u):
            return unit_at[u] // BANKS + 1

        piece_end, joint = {}, 0
        for u in UNITS:
            for q in PIECES_OF.get(u, []):
                if len(PIECES_OF[u]) == 4 and q < PIECES_OF[u][3]:
                    joint += 1
                    piece_end[q] = (joint_piece, joint)
                else:
                    v = u[:-1] + (1,) if u[0] in ("vm", "wo") else u
                    piece_end[q] = (bank_full[bank_of(v)], turn_of(v))

        LO_ENGINE = ["dve" if q < 2 else "pool" if q % 2 == 0 or MIXER_SLOTS[q // 4][0] == "br" else "dve" for q in range(4 * N_MIX)]

        def lo_engine(q):
            return LO_ENGINE[q]

        def lo_count(q, who=None):
            return LO_ENGINE[:q + 1].count(who or LO_ENGINE[q])

        def piece_views(q):
            n, j = q // 4, q % 4
            kind = MIXER_SLOTS[n][0]
            flat, hi, lo = raw[:, n % RAW, :], w_hi[:, q % SPLITS, :], w_lo[:, q % SPLITS, :]
            if kind == "br":
                k, src = H, flat.rearrange("p (k n) -> p k n", k=H)[:, :, 2 * P * j:2 * P * (j + 1)]
            elif MIXER_SLOTS[n] == ("kv", W) or kind == "wo":
                k, src = 2, flat.rearrange("p (k n) -> p k n", k=KD)[:, 2 * j:2 * j + 2, :]
            else:
                k, src = KD, flat.rearrange("p (k n) -> p k n", k=KD)[:, :, P * j:P * (j + 1)]
            return src, hi.rearrange("p (k n) -> p k n", k=k), lo.rearrange("p (k n) -> p k n", k=k)

        def as_f32(a):
            return a.bitcast(F32)

        GP, GD, GA = {}, {}, {}
        gp = gd = ga = 0
        for name in GDN_STEPS:
            gp += name != "olen"
            GP[name] = gp
            ga += {"lx0": 0, "decay": 3, "norms": 1, "tokens": 1, "kcum": 1, "olen": 1}.get(name, 1 if name.startswith(("lx", "state")) else 0)
            GA[name] = ga
            gd += {"lx0": 1, "scalars": 1, "decay": 1, "norms": 1, "lengths": 1, "scores": 1, "tokens": 1, "olen": 2}.get(
                name, 1 if name.startswith(("xlx", "vnew", "state")) else 0)
            GD[name] = gd


        def act_gdn(act, name):
            a = nc.scalar
            if name == "decay":
                act.wait_ge(g_dve, GD["decay"])
                for n in range(2):
                    a.activation(expg[:, H * n:H * n + H, :].rearrange("p a b -> p (a b)"), ps[4 + n][:, :], ACT.Exp)
                a.activation(bexp, gcum, ACT.Exp).then_inc(g_act, 1)
                a.activation(kend_s, kend_s, ACT.Exp).then_inc(g_act, 1)
                a.activation(decayT, decayT, ACT.Exp).then_inc(g_act, 1)
            elif name == "norms":
                act.wait_ge(g_pe, GP["norms"])
                a.activation(inv_norm.rearrange("p t h -> p (t h)"), ps[4][:, 0:2 * NPB], ACT.Sqrt,
                             bias=eps_rms[:, 0:1]).then_inc(g_act, 1)
            elif name == "tokens":
                act.wait_ge(g_pe, GP["tokens"])
                act.wait_ge(g_act, GA["decay"])
                for p in range(NPB):
                    ins = a.activation(kend[:, p, :], ps[4 + p // 4][:, (p % 4) * P:(p % 4 + 1) * P], ACT.Copy,
                                       scale=kend_s[:, p // H, p % H:p % H + 1])
                ins.then_inc(g_act, 1)
            elif name.startswith("lx") and name != "lx0":
                act.wait_ge(g_pe, GP[name])
                for n in range(2):
                    ins = a.copy(T1[:, H * n:H * n + H, :].rearrange("p a b -> p (a b)"), ps[4 + n][:, :])
                ins.then_inc(g_act, 1)
            elif name == "kcum":
                act.wait_ge(g_pe, GP[name])
                for n in range(2):
                    ins = a.mul(nkcT_of(n), ps[4 + n][:, :].rearrange("p (a b) -> p a b", b=P), -1.0)
                ins.then_inc(g_act, 1)
            elif name.startswith("state"):
                c = int(name[5:])
                rows = slice(CHUNK * (c % 2), CHUNK * (c % 2) + CHUNK)
                act.wait_ge(g_pe, GP[name])
                a.copy(o_tok[rows, c // 2, :], ps[7][rows, :]).then_inc(g_act, 1)
            elif name == "olen":
                act.wait_ge(g_dve, GD["state3"] + 1)
                a.activation(o_rs, o_ss, ACT.Sqrt, bias=eps_rms[:, 0:1], scale=1.0 / DH).then_inc(g_act, 1)

        def nkcT_of(t):
            return nkcT[:, :, t * P:(t + 1) * P]

        def pt4(h):
            return pT[:, 2 * (h % 2):2 * (h % 2) + 2, :]

        def pe_gdn(pe, name):
            mm, tr = nc.tensor.matmul, nc.tensor.transpose

            def out4(n):
                return ps[4 + n // 4][:, (n % 4) * P:(n % 4 + 1) * P]

            def spread(a, t, n):
                return a[:, t, n:n + 1].broadcast_to([P, P])

            def chunk_T(a, p):
                return a[:, p % H, (p // H) * P:(p // H + 1) * P]

            if name == "scalars":
                pe.wait_ge(g_dve_scal, 1)
                pe.wait_ge(consts, 3)
                mm(ps[3][:, 0:NPB], block_upper[:], g_log, start=True, stop=True)
                ins = mm(ps[3][:, NPB:2 * NPB], block_ones[:], g_log, start=True, stop=True)
            elif name == "decay":
                pe.wait_ge(g_dve, GD["scalars"])
                for p in range(NPB):
                    mm(out4(p), spread(g_log, p // H, p % H), block_upper[:], start=True, stop=True)
                for p in range(NPB):
                    ins = mm(out4(NPB + p), spread(beta, p // H, p % H), ident[:], start=True, stop=True)
            elif name == "norms":
                pe.wait_ge(g_dve_sq, 1)
                pe.wait_ge(g_dve, GD["decay"])
                pe.wait_ge(g_act, GA["decay"])
                for t in range(NT):
                    for n in range(2 * H):
                        ins = mm(ps[4][:, t * 2 * H + n:t * 2 * H + n + 1], squares[:, n, t * P:(t + 1) * P], ones[:, 0:1],
                                 start=True, stop=True)
            elif name == "lengths":
                pe.wait_ge(g_dve, GD["norms"])
                for n in range(2 * H):
                    for t in range(NT):
                        ins = mm(ps[4 + n // 2][:, (n % 2) * T + t * P:(n % 2) * T + (t + 1) * P],
                                 spread(inv_norm, t, n), ident[:], start=True, stop=True)
            elif name == "scores":
                pe.wait_ge(g_dve, GD["lengths"])
                for p in range(NPB):
                    mm(out4(p), chunk_T(kT, p), chunk_T(kT, p), start=True, stop=True)
                for p in range(NPB):
                    ins = mm(out4(NPB + p), chunk_T(kT, p), chunk_T(qT, p), start=True, stop=True)
            elif name == "tokens":
                pe.wait_ge(g_dve, GD["scores"])
                for p in range(NPB):
                    tr(out4(p), chunk_T(kT, p), ident[:])
                for p in range(NPB):
                    ins = tr(out4(NPB + p), chunk_T(vT, p), ident[:])
            elif name.startswith("lx"):
                n = int(name[2:])
                pe.wait_ge(g_pool, n + 1)
                pe.wait_ge(g_dve, GD["tokens"] if n == 0 else GD["lx0"] if n == 1 else GD[f"xlx{n - 1}"])
                pe.wait_ge(g_act, GA["tokens"])
                for p in range(NPB):
                    if n == 0:
                        ins = tr(out4(p), LTs[0][:, p, :], ident[:])
                    else:
                        ins = mm(out4(p), LTs[n % 2][:, p, :], X[:, p, :], start=True, stop=True)
            elif name.startswith("xlx"):
                n = int(name[3:])
                pe.wait_ge(g_act, GA[f"lx{n}"])
                for p in range(NPB):
                    ins = mm(out4(p), T1[:, p, :], XT[:, p, :], start=True, stop=True)
                if n < LEVELS - 1:
                    for p in range(NPB):
                        ins = mm(out4(NPB + p), XT[:, p, :], T1[:, p, :], start=True, stop=True)
            elif name == "kcum":
                pe.wait_ge(g_dve, GD[f"xlx{LEVELS - 1}"])
                for p in range(NPB):
                    ins = mm(out4(p), kbe[:, p, :], XT[:, p, :], start=True, stop=True)
            elif name.startswith("vnew"):
                c = int(name[4:])
                t, lo = c // 2, CHUNK * (c % 2)
                pe.wait_ge(g_act, GA["kcum"])
                if c:
                    pe.wait_ge(g_dve, GD[f"state{c - 1}"])
                for h in range(H):
                    o = ps[6][lo:lo + CHUNK, h * DH:(h + 1) * DH]
                    ins = mm(o, XT[:, t * H + h, lo:lo + CHUNK], vbeta[:, t * H + h, :], start=True, stop=(c == 0))
                    if c:
                        ins = mm(o, nkcT[:, h, t * P + lo:t * P + lo + CHUNK], state[:, h, :], start=False, stop=True)
            elif name.startswith("state"):
                c = int(name[5:])
                t, lo = c // 2, CHUNK * (c % 2)
                pe.wait_ge(g_dve, GD[f"vnew{c}"])
                if c:
                    pe.wait_ge(g_act, GA[f"state{c - 1}"])
                rows = slice(lo, lo + CHUNK)
                for h in range(H):
                    o = ps[7][rows, h * DH:(h + 1) * DH]
                    if c:
                        mm(o, qT[:, h, t * P + lo:t * P + lo + CHUNK], state[:, h, :], start=True, stop=False)
                    mm(o, decayT[rows, t * H + h, rows], vnew[rows, h, :], start=(c == 0), stop=True)
                for h in range(H):
                    ins = mm(ps[5][:, h * DH:(h + 1) * DH], kend[rows, t * H + h, :], vnew[rows, h, :], start=True, stop=True)
            elif name == "olen":
                return
            elif name == "onorm":
                pe.wait_ge(g_dve, GD["olen"])
                for t in range(NT):
                    for h in range(H):
                        n = h * NT + t
                        ins = tr(out4(n), o_tok[:, t, h * DH:(h + 1) * DH], ident[:])
            ins.then_inc(g_pe, 1)

        def dve_gdn(v, name, step):
            d = nc.vector

            def flat(a):
                return a.rearrange("p a b -> p (a b)")

            ident_8 = ident[:].rearrange("p (a n) -> p a n", a=1).broadcast_to([P, NPB, P])

            if name == "scalars":
                v.wait_ge(g_pe, GP[name])
                step(d.tensor_copy(gcum, ps[3][:, 0:NPB].rearrange("p (t h) -> p t h", t=NT)))
                d.tensor_tensor(kend_s, ps[3][:, NPB:2 * NPB].rearrange("p (t h) -> p t h", t=NT), gcum,
                                ALU.subtract).then_inc(g_dve, 1)
            elif name == "decay":
                v.wait_ge(g_pe, GP[name])
                for p in range(NPB):
                    d.scalar_tensor_tensor(out=decayT[:, p, :], in0=ps[4 + p // 4][:, (p % 4) * P:(p % 4 + 1) * P],
                                           scalar=gcum[:, p // H, p % H:p % H + 1], in1=negmask[:],
                                           op0=ALU.subtract, op1=ALU.add)
                for n in range(2):
                    ins = d.tensor_copy(flat(LT[:, H * n:H * n + H, :]), ps[6 + n][:, :])
                ins.then_inc(g_dve, 1)
            elif name == "norms":
                v.wait_ge(g_act, GA["decay"])
                step(d.tensor_tensor(bexp, bexp, beta, ALU.mult))
                step(d.tensor_copy(chunk_decay, expg[:, :, CHUNK - 1::CHUNK]))
                v.wait_ge(g_act, GA[name])
                d.reciprocal(inv_norm, inv_norm).then_inc(g_dve, 1)
            elif name == "lengths":
                v.wait_ge(g_pe, GP[name])
                for n in range(2):
                    o = flat(kT)[:, 512 * n:512 * n + 512]
                    d.tensor_tensor(o, o, ps[6 + n][:, :], ALU.mult)
                for n in range(2):
                    o = flat(qT)[:, 512 * n:512 * n + 512]
                    ins = d.scalar_tensor_tensor(out=o, in0=o, scalar=DH ** -0.5, in1=ps[4 + n][:, :],
                                                 op0=ALU.mult, op1=ALU.mult)
                ins.then_inc(g_dve, 1)
            elif name == "scores":
                v.wait_ge(g_pe, GP[name])
                step(d.tensor_tensor(LT, LT, decayT, ALU.mult))
                for n in range(2):
                    o = flat(LT[:, H * n:H * n + H, :])
                    step(d.tensor_tensor(o, o, ps[4 + n][:, :], ALU.mult))
                for n in range(2):
                    o = flat(decayT[:, H * n:H * n + H, :])
                    step(d.tensor_tensor(o, o, ps[6 + n][:, :], ALU.mult))
                qv = qT.rearrange("p h (t n) -> p t h n", t=NT)
                ev = expg.rearrange("p (t h) n -> p t h n", t=NT)
                for t in range(NT):
                    ins = d.tensor_tensor(qv[:, t, :, :], qv[:, t, :, :], ev[:, t, :, :], ALU.mult)
                ins.then_inc(g_dve, 1)
            elif name == "tokens":
                v.wait_ge(g_pe, GP[name])
                def scaled(out, n, t, by):
                    by = by[:, t, :].rearrange("p (h a) -> p h a", a=1).broadcast_to([P, H, P])
                    return d.tensor_tensor(out[:, t * H:(t + 1) * H, :], ps[n][:, :].rearrange("p (h n) -> p h n", h=H), by, ALU.mult)

                for t in range(NT):
                    scaled(vbeta, 6 + t, t, beta)
                v.wait_ge(g_act, GA[name])
                for t in range(NT):
                    ins = scaled(kbe, 4 + t, t, bexp)
                ins.then_inc(g_dve, 1)
            elif name == "lx0":
                v.wait_ge(g_pool, 1)
                d.tensor_tensor(XT, ident_8, LTs[0], ALU.subtract)
                v.wait_ge(g_pe, GP[name])
                for n in range(2):
                    ins = d.tensor_tensor(X[:, H * n:H * n + H, :], ident_8[:, 0:H, :],
                                          ps[4 + n][:, :].rearrange("p (a n) -> p a n", a=H), ALU.subtract)
                ins.then_inc(g_dve, 1)
            elif name.startswith("xlx"):
                v.wait_ge(g_pe, GP[name])
                last = int(name[3:]) == LEVELS - 1
                for n in range(2):
                    o = flat(XT[:, H * n:H * n + H, :])
                    ins = d.tensor_tensor(o, o, ps[4 + n][:, :], ALU.subtract)
                if not last:
                    for n in range(2):
                        o = flat(X[:, H * n:H * n + H, :])
                        ins = d.tensor_tensor(o, o, ps[6 + n][:, :], ALU.subtract)
                ins.then_inc(g_dve, 1)
            elif name.startswith("vnew"):
                c = int(name[4:])
                rows = slice(CHUNK * (c % 2), CHUNK * (c % 2) + CHUNK)
                v.wait_ge(g_pe, GP[name])
                d.tensor_copy(flat(vnew)[rows, :], ps[6][rows, :]).then_inc(g_dve, 1)
            elif name.startswith("state"):
                c = int(name[5:])
                rows = slice(CHUNK * (c % 2), CHUNK * (c % 2) + CHUNK)
                v.wait_ge(g_pe, GP[name])
                for h in range(H):
                    o = ps[5][:, h * DH:(h + 1) * DH]
                    if c == 0:
                        ins = d.tensor_copy(state[:, h, :], o)
                    else:
                        ins = d.scalar_tensor_tensor(out=state[:, h, :], in0=state[:, h, :],
                                                     scalar=chunk_decay[:, (c // 2) * H + h, c % 2:c % 2 + 1],
                                                     in1=o, op0=ALU.mult, op1=ALU.add)
                ins.then_inc(g_dve, 1)
                v.wait_ge(g_dve, GD[name])
            elif name == "olen":
                v.wait_ge(g_act, GA["state3"])
                of = o_tok.rearrange("p t (h n) -> p (t h) n", h=H)
                step(d.tensor_tensor(LT, of, of, ALU.mult))
                d.tensor_reduce(o_ss, LT, AX.X, ALU.add).then_inc(g_dve, 1)
                v.wait_ge(g_act, GA[name])
                step(d.reciprocal(o_rs, o_rs))
                d.tensor_tensor(of, of, o_rs.rearrange("p (a b) -> p a b", b=1).broadcast_to([P, NPB, P]),
                                ALU.mult).then_inc(g_dve, 1)
            elif name == "onorm":
                v.wait_ge(g_pe, GP[name])
                for n in range(2):
                    ins = d.scalar_tensor_tensor(out=flat(yaT)[:, 512 * n:512 * n + 512], in0=ps[4 + n][:, :],
                                                 scalar=small_cols[:, 60:61], in1=flat(zs)[:, 512 * n:512 * n + 512],
                                                 op0=ALU.mult, op1=ALU.mult)
                ins.then_inc(ya_ready, 1)

        def wait_copied(eng, kind, count):
            units = [u for u in UNITS if u[0] == kind][:count]
            for b in range(BANKS):
                turns = [turn_of(u) for u in units if bank_of(u) == b]
                if turns:
                    eng.wait_ge(bank_free[b], max(turns))

        def prep_lo(eng, ops, q, who):
            if lo_engine(q) == who:
                src, hi, lo = piece_views(q)
                eng.wait_ge(split_hi, q + 1)
                ops.tensor_tensor(lo, src, as_f32(hi), ALU.subtract).then_inc(split_lo[who], 1)

        def slot_dma(sp, n):
            kind, c = MIXER_SLOTS[n]
            dst = raw[:, n % RAW, :]
            if kind == "br":
                dst, src = dst.rearrange("p (k n) -> p k n", k=H), w_br[0, c].rearrange("(k p) n -> p k n", p=P)
            else:
                m = {"kv": w_mem_kv, "in": w_in, "wo": w_o}[kind][0]
                dst = dst.rearrange("p (k n) -> p k n", k=KD)
                src = m.rearrange("(k p) n -> p k n", p=P)[:, :, c:c + W]
            if n >= RAW:
                raw_spent(sp, n - RAW)
            if n == 0:
                for j in range(4):
                    sp.dma_start(dst[:, :, j * P:(j + 1) * P], src[:, :, j * P:(j + 1) * P]).then_inc(piece_in[j], 16)
            else:
                sp.dma_start(dst, src).then_inc(raw_in[n % RAW], 16)

        def raw_spent(sp, n):
            for who in split_lo:
                sp.wait_ge(split_lo[who], lo_count(4 * n + 3, who))

        def chunk_dma(sp, c, gu, dn, dst, landed):
            if c < 4:
                src = gu.rearrange("(k p) n -> p k n", p=P)[:, 2 * c:2 * c + 2, :]
                dst = dst.rearrange("p (k n) -> p k n", k=2)
            else:
                src = dn.rearrange("(k p) n -> p k n", p=P)[:, 4 * (c - 4):4 * (c - 4) + 4, :]
                dst = dst.rearrange("p (k n) -> p k n", k=4)
            sp.dma_start(dst, src).then_inc(landed, 16)

        RING_IN = raw_in + first_in + late_in
        MIXER_FILLS = [len(range(r or RAW, N_MIX, RAW)) if r < RAW else 0 for r in range(RING)]

        def ring_place(m, rounds=0):
            r = m % RING
            fill = m // RING + 1 + MIXER_FILLS[r]
            return RING_SLOTS[r], RING_IN[r], (rounds * (ROUND * EC // RING) + fill) * 16

        def item_places(i, rounds=0):
            return [ring_place(EC * i + c, rounds) for c in range(EC)]

        def further_places(i):
            return [(slot, landed, 16 * i + (count - 16 * (NE - 1))) for slot, landed, count in item_places(NE - 1)]

        def chunk_spent(eng, m, items=0):
            i, c = items + m // EC, m % EC
            if c == 3:
                eng.wait_ge(gu_done, i + 1)
            elif c == 5:
                eng.wait_ge(down_done, i + 1)
            else:
                eng.wait_ge(chunks_used, 4 * i + (c + 1 if c < 3 else 4))

        block = ctx.enter_context(nc.Block())

        @block.sync
        def _(sp):
            def bcast(dst, src, done):
                sp.dma_start(dst, src).then_inc(done, 16)

            sp.dma_start(mem_tok, mem[0].rearrange("(t p) d -> p t d", p=P)).then_inc(mem_in, 16)
            slot_dma(sp, 0)
            sp.dma_start(hx[:], x[0].rearrange("(t p) d -> p t d", p=P)).then_inc(x_in, 16)
            bcast(lnp0[:, 0, :], ln0_g.rearrange("(a d) -> a d", a=1).broadcast_to([P, D]), lnp_in[0])
            bcast(lnp0[:, 1, :], ln0_b.rearrange("(a d) -> a d", a=1).broadcast_to([P, D]), lnp_in[0])
            for n in range(1, N_MIX):
                slot_dma(sp, n)
            sp.wait_ge(ya_split, 1)
            sp.wait_ge(yb_split, 1)
            sp.dma_start(bgu[0:NE, :], b_gate_up[0]).then_inc(ebias_in, 16)
            sp.dma_start(bdown[0:NE, :], b_down[0]).then_inc(ebias_in, 16)
            bcast(lnp1[:, 0, :], ln1_g.broadcast_to([P, D]), lnp_in[1])
            bcast(lnp1[:, 1, :], ln1_b.broadcast_to([P, D]), lnp_in[1])
            order = list(range(RAW, EC)) + list(range(RAW))
            for c in order:
                if c < RAW:
                    raw_spent(sp, N_MIX - RAW + (c - N_MIX) % RAW)
                chunk_dma(sp, c, w_gate_up[0, 0], w_down[0, 0], *ring_place(c)[0:2])
            sp.wait_ge(bank_full[bank_of(("wo", 1, 1))], turn_of(("wo", 1, 1)))
            for c in range(EC):
                if EC + c == RING - 1:
                    sp.wait_ge(bank_full[bank_of(("logits", 1))], turn_of(("logits", 1)))
                if EC + c >= RING:
                    chunk_spent(sp, EC + c - RING)
                chunk_dma(sp, c, w_gate_up[0, 1], w_down[0, 1], *ring_place(EC + c)[0:2])
            with sp.Fori(0, ROUNDS) as j:
                for u in range(ROUND):
                    ex = ROUND * j + (2 + u)
                    gu = w_gate_up[0, bass.ds(ex, 1), :, :].rearrange("e d f -> (e d) f")
                    dn = w_down[0, bass.ds(ex, 1), :, :].rearrange("e d f -> (e d) f")
                    for c in range(EC):
                        m = EC * (2 + u) + c
                        chunk_spent(sp, m - RING, ROUND * j)
                        chunk_dma(sp, c, gu, dn, *ring_place(m)[0:2])
            chunk_spent(sp, LAST_IN_LN2_SLOT)
            bcast(lnp2[:, 0, :], ln2_g.broadcast_to([P, D]), lnp_in[2])
            bcast(lnp2[:, 1, :], ln2_b.broadcast_to([P, D]), lnp_in[2])
            sp.wait_ge(r_items, 1)
            n_items = sp.value_load(count_i[0:1, 0:1], min_val=NE, max_val=NE + EXTRA)
            with sp.If_ne(sp.to_reg(n_items), NE):
                with sp.Fori(NE, n_items) as i:
                    ex = sp.value_load(ids_i[0:1, bass.ds(i, 1)], min_val=0, max_val=NE - 1)
                    gu = w_gate_up[0, bass.ds(ex, 1), :, :].rearrange("e d f -> (e d) f")
                    dn = w_down[0, bass.ds(ex, 1), :, :].rearrange("e d f -> (e d) f")
                    for c in range(EC):
                        chunk_spent(sp, c, i - 1)
                        chunk_dma(sp, c, gu, dn, *further_places(i)[c][0:2])
            for t in range(NT):
                for c in range(2):
                    sp.wait_ge(half_out, 2 * t + c + 1)
                    sp.dma_start(out[0, t * P:(t + 1) * P, 512 * c:512 * c + 512],
                                 hx[:, t, 512 * c:512 * c + 512]).then_inc(out_stored, 16)
            sp.wait_ge(out_stored, 16 * 2 * NT)

        @block.gpsimd
        def _(pool):
            chain = [0]

            def step(ins):
                chain[0] += 1
                ins.then_inc(pool_chain, 1)
                pool.wait_ge(pool_chain, chain[0])

            eng = nc.gpsimd
            step(eng.memset(ones[:], 1.0))
            eng.affine_select(out=ident[:], in_=ones[:], pattern=[[-1, P]], compare_op=ALU.is_equal,
                              fill=0.0, base=0, channel_multiplier=1).then_inc(consts, 1)
            eng.memset(eps_ln, LN_EPS)
            eng.memset(eps_rms, RMS_EPS).then_inc(consts, 1)
            eng.memset(qkv_pad[:, :, 0:3], 0.0)
            eng.memset(upad[:, :, 0:2], 0.0).then_inc(pads, 1)

            def masks():
                eng.affine_select(out=before[:], in_=ones[:], pattern=[[1, P]], compare_op=ALU.is_gt,
                                  fill=0.0, base=0, channel_multiplier=-1)
                for n in range(LEVELS + 1):
                    s = 1 << n
                    v = blocks[:, n, :].rearrange("p (b s) -> p b s", s=s)
                    o = ones[:].rearrange("p (b s) -> p b s", s=s)
                    step(eng.affine_select(out=v, in_=o, pattern=[[-s, P // s], [0, s]],
                                           compare_op=ALU.is_ge, fill=0.0, base=0, channel_multiplier=1))
                    step(eng.affine_select(out=v, in_=v, pattern=[[s, P // s], [0, s]],
                                           compare_op=ALU.is_ge, fill=0.0, base=s - 1, channel_multiplier=-1))
                eng.tensor_scalar(alpha_ident[:], ident[:], ALPHA, None, ALU.mult)
                step(eng.tensor_copy(block_ones[:], blocks[:, LEVELS, :]))
                step(eng.affine_select(out=block_upper[:], in_=block_ones[:], pattern=[[1, P]],
                                       compare_op=ALU.is_ge, fill=0.0, base=0, channel_multiplier=-1))
                step(eng.tensor_scalar(negmask[:], block_upper[:], -1.0, BIG, ALU.add, ALU.mult))
                for n in range(LEVELS):
                    step(eng.tensor_tensor(level_mask[:, n, :], blocks[:, n + 1, :], blocks[:, n, :], ALU.subtract))
                for n in range(LEVELS):
                    ins = eng.affine_select(out=level_mask[:, n, :], in_=level_mask[:, n, :], pattern=[[1, P]],
                                            compare_op=ALU.is_gt, fill=0.0, base=0, channel_multiplier=-1)
                ins.then_inc(consts, 1)

            masks()
            MASK_LEVEL = {("g", "tokens"): 0}
            MASK_LEVEL.update({("g", f"lx{n - 1}"): n for n in range(1, LEVELS)})
            for s in SCHEDULE:
                if s[0] == "prep":
                    prep_lo(pool, eng, s[1], "pool")
                if s in MASK_LEVEL:
                    n = MASK_LEVEL[s]
                    if n == 0:
                        pool.wait_ge(g_dve, GD["scores"])
                    if n >= 2:
                        pool.wait_ge(g_pe, GP[f"lx{n - 2}"])
                    if n == 2:
                        pool.wait_ge(g_dve, GD["lx0"])
                    m = level_mask[:, n:n + 1, :].broadcast_to([P, NPB, P])
                    eng.tensor_tensor(LTs[n % 2], LT, m, ALU.mult).then_inc(g_pool, 1)
            pool.wait_ge(sum_split, KD)
            eng.iota(slot_iota.rearrange("p (a b) -> p a b", b=CAP), pattern=[[0, 2], [1, CAP]], base=0,
                     channel_multiplier=0, allow_small_or_imprecise_dtypes=True)
            eng.iota(part_iota, pattern=[[0, P]], base=0, channel_multiplier=1,
                     allow_small_or_imprecise_dtypes=True)
            eng.iota(e_iota, pattern=[[1, NE]], base=0, channel_multiplier=0,
                     allow_small_or_imprecise_dtypes=True)
            eng.memset(ranks, NOT_HERE)
            eng.memset(weights, 0.0)
            eng.memset(ids, 0.0).then_inc(moe_consts, 1)
            pool.wait_ge(lnp_in[1], 32)
            for t in range(NT):
                pool.wait_ge(bank_full[bank_of(("x1T", t, 1))], turn_of(("x1T", t, 1)))
                step(eng.tensor_tensor(hx[:, t, :], hx[:, t, :], lnp1[:, 0, :], ALU.mult))
                eng.tensor_tensor(hx[:, t, :], hx[:, t, :], lnp1[:, 1, :], ALU.add).then_inc(x1_ready, 1)

        @block.scalar
        def _(act):
            chain = [0]
            a = nc.scalar

            def step(ins):
                chain[0] += 1
                ins.then_inc(act_chain, 1)
                act.wait_ge(act_chain, chain[0])

            rows = small_rows
            act.dma_start(rows[0:48, :], conv_qkv[0].rearrange("j (c p) -> (j c) p", p=P)).then_inc(rows_in, 16)
            act.dma_start(rows[48:60, :], conv_mix[0].rearrange("j (c p) -> (j c) p", p=P)).then_inc(rows_in, 16)
            act.dma_start(rows[ROW_NORM:ROW_G, :], gdn_norm).then_inc(rows_in, 16)
            act.dma_start(rows[ROW_G:ROW_B, :], ln1_g[0].rearrange("(c p) -> c p", p=P)).then_inc(rows_in, 16)
            act.dma_start(rows[ROW_B:N_ROWS, :], ln1_b[0].rearrange("(c p) -> c p", p=P)).then_inc(rows_in, 16)
            act.dma_start(w_ab, w_in[0].rearrange("(k p) n -> p k n", p=P)[:, :, C_AB:C_AB + 2 * H]).then_inc(ab_in, 16)
            act.dma_start(adt[:, 0, :], a_log.broadcast_to([P, H])).then_inc(adt_in, 16)
            act.dma_start(adt[:, 1, :], dt_bias.broadcast_to([P, H])).then_inc(adt_in, 16)
            act.dma_start(wr[:], w_router[0].rearrange("(k p) e -> p k e", p=P)).then_inc(router_in, 16)
            act.dma_start(br_bc[:], b_router.broadcast_to([P, NE])).then_inc(router_in, 16)

            def ln_root_of(n, t):
                act.wait_ge(ln_var, NT * n + t + 1)
                a.activation(ln_std[:, t:t + 1], ln_mv[:, t, 1:2], ACT.Sqrt, bias=eps_ln[:, 0:1]).then_inc(ln_root, 1)

            def bank(u, n=T):
                return ps[bank_of(u)][:, 0:n]

            def silu(n):
                act.wait_ge(conv_done, n + 1)
                a.activation(qkvT[:, n, :], qkvT[:, n, :], ACT.Silu).then_inc(silu_done, 1)

            act.wait_ge(consts, 2)
            a.copy(ln_std[:, 0:1], eps_ln)
            for s in SCHEDULE:
                kind = s[0]
                if kind in ("memT", "hT", "km", "vm", "z", "xc", "gb", "qm", "gate", "qkv", "pT", "ym", "x1T"):
                    act.wait_ge(bank_full[bank_of(s)], turn_of(s))
                free = bank_free[bank_of(s)] if kind not in NOT_UNITS else None
                if kind == "prep":
                    q = s[1]
                    n = q // 4
                    if n == 0:
                        act.wait_ge(piece_in[q], 16)
                    else:
                        act.wait_ge(raw_in[n % RAW], 16 * len(range(n % RAW or RAW, n + 1, RAW)))
                    if q >= SPLITS:
                        act.wait_ge(*piece_end[q - SPLITS])
                        act.wait_ge(split_lo[lo_engine(q - SPLITS)], lo_count(q - SPLITS))
                    src, hi, _ = piece_views(q)
                    a.copy(hi, src).then_inc(split_hi, 1)
                elif kind == "memT":
                    a.copy(src_hi[:, 2 * s[1]:2 * s[1] + 2, :], bank(s, 512).rearrange("p (a b) -> p a b", a=2)).then_inc(bank_hi, 1)
                elif kind == "hT":
                    t, j = s[1:]
                    a.copy(act_hi[:, 4 * j:4 * j + 4, t * P:(t + 1) * P],
                           bank(s, 512).rearrange("p (a b) -> p a b", b=P)).then_inc(bank_hi, 1)
                elif kind == "ln":
                    ln_root_of(*s[1:])
                elif kind == "km":
                    a.copy(kmT[:, s[1], :], bank(s)).then_inc(free, 1)
                elif kind == "vm":
                    a.copy(vm[:, s[1], :], bank(s, 512)).then_inc(free, 1)
                elif kind == "qkv":
                    if s[1] == 0:
                        act.wait_ge(pads, 1)
                    a.copy(qkv_pad[:, s[1], 3:3 + T], bank(s)).then_inc(free, 1)
                    if s[1] >= 1:
                        silu(s[1] - 1)
                    if s[1] == 11:
                        silu(11)
                elif kind == "abT":
                    act.wait_ge(ab_dve, 1)
                    step(a.activation(t_b, t_b, ACT.Exp))
                    step(a.activation(ea, adt[:, 0, :], ACT.Exp))
                    a.activation(t_b, t_b, ACT.Ln, bias=1.0).then_inc(ab_act, 1)
                    a.activation(beta, beta, ACT.Sigmoid).then_inc(ab_act, 1)
                elif kind == "z":
                    a.activation(zs[:, s[1], :], bank(s), ACT.Silu).then_inc(free, 1)
                elif kind == "xc":
                    a.copy(xc[:, s[1], :], bank(s)).then_inc(free, 1)
                elif kind == "gb":
                    a.copy(gb[:, s[1], :], bank(s)).then_inc(free, 1)
                elif kind == "qm":
                    a.copy(qm[:, s[1], :], bank(s)).then_inc(free, 1)
                    if s[1] == 0:
                        act.wait_ge(yb_ready, 1)
                        wait_copied(act, "vm", 2)
                        a.copy(src_hi[:, H:2 * H, :], xc).then_inc(yb_hi, 1)
                elif kind == "score":
                    act.wait_ge(att_max, s[1] + 1)
                    for t in range(NT):
                        ins = a.activation(probs[:, s[1], t, :], ps[bank_of(s)][:, t * T:(t + 1) * T], ACT.Exp,
                                           bias=s_neg[:, s[1], t:t + 1], scale=DH ** -0.5,
                                           accum_out=s_sum[:, s[1], t:t + 1])
                    ins.then_inc(free, 1)
                elif kind == "pT":
                    a.copy(pt4(s[1]).rearrange("p a b -> p (a b)"), bank(s, 512)).then_inc(free, 1)
                elif kind == "ym":
                    a.copy(src_hi[:, s[1], :], bank(s)).then_inc(bank_hi, 1)
                elif kind == "gate":
                    b, c = s[1:]
                    if b == 2:
                        if c == 0:
                            act.wait_ge(yb_split, 1)
                        dst = first_gates[:, c, :]
                    elif b == 1:
                        dst = gates[:, c, :]
                    else:
                        act.wait_ge(gate_used, c + 1)
                        dst = gates[:, c, :]
                    a.activation(dst, bank(s), ACT.Sigmoid).then_inc(free, 1)
                elif kind == "ya":
                    act.wait_ge(ya_ready, 1)
                    act.wait_ge(bank_full[bank_of(("br", 2, KD - 1))], turn_of(("br", 2, KD - 1)))
                    a.copy(src_hi[:, 0:H, :], yaT).then_inc(ya_hi, 1)
                elif kind == "sum hi":
                    act.wait_ge(sum_ready, s[1] + 1)
                    a.copy(act_hi[:, s[1], :], merged[:, s[1], :]).then_inc(sum_hi, 1)
                elif kind == "x1T":
                    t, j = s[1:]
                    if j == 0:
                        for k in range(4):
                            ins = a.activation(x1T[:, k, t * P:(t + 1) * P], ps[bank_of(s)][:, k * P:(k + 1) * P],
                                               ACT.Identity, scale=small_cols[:, ROW_G + k:ROW_G + k + 1],
                                               bias=small_cols[:, ROW_B + k:ROW_B + k + 1])
                        ins.then_inc(free, 1)
                elif kind == "logits":
                    t = s[1]
                    act.wait_ge(r_max, t + 1)
                    a.activation(el[:, t, :], logits[:, t, :], ACT.Exp, bias=r_neg[:, t:t + 1])
                    a.activation(top_e[:, t, 0:TOPK], top_v[:, t, 0:TOPK], ACT.Exp,
                                 bias=r_neg[:, t:t + 1], accum_out=r_sum[:, t:t + 1]).then_inc(r_exp, 1)
                elif kind == "g":
                    act_gdn(act, s[1])

            def item(i):
                act.wait_ge(gate_cut, i + 1)
                a.activation(sig1, gate1, ACT.Sigmoid, scale=SWIGLU_ALPHA).then_inc(sig_done, 1)
                act.wait_ge(hid_turned, i + 1)
                a.copy(hidT.rearrange("p a b -> p (a b)"), ps[3][:, :]).then_inc(hid_copied, 1)
                act.wait_ge(down_done, i + 1)
                a.copy(y_tok[0:64, :], ps[3][0:64, :]).then_inc(y_copied, 1)

            item(0)
            act.wait_ge(r_items, 1)
            n_items = act.value_load(count_i[0:1, 0:1], min_val=NE, max_val=NE + EXTRA)
            with act.Fori(1, n_items) as i:
                item(i)
            for t in range(NT):
                ln_root_of(2, t)

        @block.tensor
        def _(pe):
            mm = nc.tensor.matmul
            tr = nc.tensor.transpose

            def piece(q):
                pe.wait_ge(split_lo[lo_engine(q)], lo_count(q))
                _, hi, lo = piece_views(q)
                return hi, lo

            def three(o, l_hi, l_lo, r_hi, r_lo, start, stop):
                mm(o, l_hi, r_hi, start=start, stop=False)
                mm(o, l_hi, r_lo, start=False, stop=False)
                return mm(o, l_lo, r_hi, start=False, stop=stop)

            def project(s, rhs_hi, rhs_lo, c=0, nk=KD):
                hi, lo = piece(PIECES_OF[s][-1])
                for k in range(nk):
                    ins = three(ps[bank_of(s)][:, 0:T], hi[:, k, c * P:(c + 1) * P], lo[:, k, c * P:(c + 1) * P],
                                rhs_hi[:, k, :], rhs_lo[:, k, :], k == 0, k == nk - 1)
                ins.then_inc(bank_full[bank_of(s)], 1)

            def project_rows(s, lhs_hi, lhs_lo, sums=False):
                both = [s, s[:-1] + (1,)]
                for j, q in enumerate(PIECES_OF[s]):
                    hi, lo = piece(q)
                    if sums:
                        pe.wait_ge(sum_split, 2 * j + 2)
                    for kk in range(2):
                        k = 2 * j + kk
                        for t, u in enumerate(both):
                            ins = three(ps[bank_of(u)][:, :], lhs_hi[:, k, t * P:(t + 1) * P], lhs_lo[:, k, t * P:(t + 1) * P],
                                        hi[:, kk, :], lo[:, kk, :], k == 0, k == KD - 1)
                            if k == KD - 1:
                                ins.then_inc(bank_full[bank_of(u)], 1)
                    if j < 3:
                        ins.then_inc(joint_piece, 1)

            pe.wait_ge(consts, 1)
            for s in SCHEDULE:
                kind = s[0]
                if kind == "g":
                    pe_gdn(pe, s[1])
                if kind in NOT_UNITS:
                    continue
                b = bank_of(s)
                bk = ps[b]
                for u in ([s, s[:-1] + (1,)] if kind in ("vm", "wo") and s[-1] == 0 else [s]):
                    if unit_at[u] >= BANKS:
                        pe.wait_ge(bank_free[bank_of(u)], turn_of(u) - 1)
                if kind == "memT":
                    if s[1] == 0:
                        pe.wait_ge(mem_in, 16)
                    for k in range(2):
                        for t in range(NT):
                            ins = tr(bk[:, k * T + t * P:k * T + (t + 1) * P],
                                     mem_tok[:, t, (2 * s[1] + k) * P:(2 * s[1] + k + 1) * P], ident[:])
                    ins.then_inc(bank_full[b], 1)
                elif kind == "km":
                    if s[1] == 0:
                        wait_copied(pe, "memT", 4)
                    project(s, src_hi, src_lo)
                elif kind == "vm":
                    if s[1] == 0:
                        project_rows(s, src_hi, src_lo)
                elif kind in ("hT", "x1T"):
                    t, j = s[1:]
                    pe.wait_ge(ln_done, t + 1 if kind == "hT" else NT + t + 1)
                    for k in range(4):
                        ins = tr(bk[:, k * P:(k + 1) * P], hx[:, t, (4 * j + k) * P:(4 * j + k + 1) * P], ident[:])
                    ins.then_inc(bank_full[b], 1)
                elif kind == "ab":
                    pe.wait_ge(rows_in, 80)
                    tr(ps[3][:, 0:N_ROWS], small_rows[:, :], ident[0:N_ROWS, 0:N_ROWS]).then_inc(cols_turned, 1)
                    wait_copied(pe, "hT", 4)
                    pe.wait_ge(ab_split, 2)
                    for k in range(KD):
                        ins = three(bk[0:2 * H, 0:T], w_ab_hi[:, k, :], w_ab_lo[:, k, :], act_hi[:, k, :], act_lo[:, k, :],
                                    k == 0, k == KD - 1)
                    ins.then_inc(bank_full[b], 1)
                elif kind == "abT":
                    pe.wait_ge(bank_free[bank_of(("ab", 0))], turn_of(("ab", 0)))
                    for t in range(NT):
                        ins = tr(bk[:, t * 2 * H:(t + 1) * 2 * H], ab_rows[0:2 * H, t * P:(t + 1) * P], ident[0:2 * H, 0:2 * H])
                    ins.then_inc(bank_full[b], 1)
                elif kind in ("qkv", "z", "xc", "gc", "gb", "qm", "gate"):
                    project(s, act_hi, act_lo)
                elif kind == "score":
                    wait_copied(pe, "qm", s[1] + 1)
                    for t in range(NT):
                        ins = mm(bk[:, t * T:(t + 1) * T], qm[:, s[1], t * P:(t + 1) * P], kmT[:, s[1], :],
                                 start=True, stop=True)
                    ins.then_inc(bank_full[b], 1)
                elif kind == "pT":
                    pe.wait_ge(att_p, s[1] + 1)
                    for m in range(2):
                        for t in range(NT):
                            ins = tr(bk[:, m * T + t * P:m * T + (t + 1) * P], probs[:, s[1], t, m * P:(m + 1) * P], ident[:])
                    ins.then_inc(bank_full[b], 1)
                elif kind == "ym":
                    wait_copied(pe, "pT", s[1] + 1)
                    for m in range(2):
                        ins = mm(bk[:, 0:T], vm[:, m, s[1] * DH:(s[1] + 1) * DH], pt4(s[1])[:, m, :],
                                 start=(m == 0), stop=(m == 1))
                    ins.then_inc(bank_full[b], 1)
                elif kind == "br":
                    if s[2] == 0:
                        if s[1] == 2:
                            wait_copied(pe, "ym", 4)
                        if s[1] == 1:
                            pe.wait_ge(yb_split, 1)
                        if s[1] == 0:
                            pe.wait_ge(ya_split, 1)
                    f = H if s[1] == 1 else 0
                    project(s, src_hi[:, f:f + H, :], src_lo[:, f:f + H, :], c=s[2] % 2, nk=H)
                elif kind == "wo":
                    if s[2] == 0:
                        project_rows(s, act_hi, act_lo, s[1] == 0)
                elif kind == "logits":
                    t = s[1]
                    wait_copied(pe, "x1T", 2 * t + 2)
                    pe.wait_ge(router_in, 32)
                    for k in range(KD):
                        ins = mm(bk[:, 0:NE], x1T[:, k, t * P:(t + 1) * P], wr[:, k, :], start=(k == 0), stop=(k == KD - 1))
                    ins.then_inc(bank_full[b], 1)
                elif kind == "rank":
                    pe.wait_ge(r_mask, 1)
                    mm(bk[:, 0:NE], before[:], mask[:, 0, :], start=True, stop=True)
                    mm(bk[:, NE:2 * NE], ones[:], mask[:, 0, :], start=True, stop=False)
                    mm(bk[:, NE:2 * NE], before[:], mask[:, 1, :], start=False, stop=True)
                    for t in range(NT):
                        ins = mm(bk[0:NE, 2 * NE:2 * NE + 1], mask[:, t, :], ones[:, 0:1], start=(t == 0), stop=(t == 1))
                    ins.then_inc(bank_full[b], 1)

            def residual(t):
                for c in range(2):
                    mm(ps[4 + 2 * t + c][:, :], alpha_ident[:], hx[:, t, c * 512:(c + 1) * 512],
                       start=(t == 0), stop=True, skip_group_check=True)

            def gather(first=0, last=KD):
                for k in range(first, last):
                    for t in range(NT):
                        ins = mm(ps[0][:, k * CAP:(k + 1) * CAP], hx[:, t, k * P:(k + 1) * P], onehot[:, t, :],
                                 start=(t == 0), stop=(t == NT - 1))
                if last == KD:
                    ins.then_inc(gathered, 1)

            def bias():
                for bk, at in ((ps[1], 0), (ps[2], FF)):
                    for c in range(2):
                        mm(bk[64 * c:64 * c + 64, :], e_row[0:NE, :], bgu[0:NE, at + 512 * c:at + 512 * (c + 1)],
                           start=True, stop=False)

            def gate_up(i, places, amid=True):
                pe.wait_ge(tokens_in, i + 1)
                if amid:
                    bias()
                for q in range(4):
                    slot, landed, count = places[q]
                    pe.wait_ge(landed, count)
                    w = slot.rearrange("p (k n) -> p k n", k=2)
                    for kk in range(2):
                        k = 2 * q + kk
                        for bk, at in ((ps[1], 0), (ps[2], FF)):
                            for c in range(2):
                                ins = mm(bk[64 * c:64 * c + 64, :], x_slotT[:, k, :],
                                         w[:, kk, at + 512 * c:at + 512 * (c + 1)], start=False, stop=(k == KD - 1))
                    ins.then_inc(chunks_used if q < 3 else gu_done, 1)
                    if amid and q == 0:
                        turn_scatter(i - 1)
                    if amid and q == 1:
                        pe.wait_ge(onehots, i + 2)
                        gather(0, 2)
                    if amid and q == 2:
                        gather(2, 6)

            def turn_hidden(i):
                pe.wait_ge(hid_done, i + 1)
                for c in range(4):
                    ins = tr(ps[3][:, c * P:(c + 1) * P], h_tok[:, c * P:(c + 1) * P], ident[:])
                ins.then_inc(hid_turned, 1)

            def down(i, places):
                pe.wait_ge(hid_copied, i + 1)
                for q in range(2):
                    slot, landed, count = places[4 + q]
                    pe.wait_ge(landed, count)
                    w = slot.rearrange("p (k n) -> p k n", k=4)
                    for kk in range(4):
                        for c in range(2):
                            ins = mm(ps[3][64 * c:64 * c + 64, :], hidT[:, kk, 64 * q:64 * q + 64],
                                     w[:, kk, c * 512:(c + 1) * 512], start=(q == 0 and kk == 0), stop=(q == 1 and kk == 3))
                    ins.then_inc(chunks_used if q < 1 else down_done, 1)

            def turn_scatter(i):
                pe.wait_ge(y_copied, 2 * i + 2)
                for t in range(NT):
                    ins = tr(ps[3][:, t * P:(t + 1) * P], onehot_w[:, t, :], ident[:])
                ins.then_inc(sc_turned, 1)

            def scatter_tile(t):
                for c in range(2):
                    ins = mm(ps[4 + 2 * t + c][:, :], scatter[64 * c:64 * c + 64, t * P:(t + 1) * P],
                             y_tok[64 * c:64 * c + 64, :], start=False, stop=True, skip_group_check=True)
                return ins

            def scatter_add(i):
                pe.wait_ge(sc_copied, i + 1)
                for t in range(NT):
                    scatter_tile(t)

            pe.wait_ge(bank_free[bank_of(("rank", 0))], turn_of(("rank", 0)))
            pe.wait_ge(x1_ready, 2)
            residual(0)
            pe.wait_ge(onehots, 1)
            gather()
            pe.wait_ge(ebias_in, 32)
            bias()
            gate_up(0, item_places(0), amid=False)
            pe.wait_ge(onehots, 2)
            gather()
            for t in range(NT):
                tr(ps[7][0:NE, t * P:(t + 1) * P], ranks[:, t, 0:NE], ident[:])
            for t in range(NT):
                ins = tr(ps[7][0:NE, T + t * P:T + (t + 1) * P], weights[:, t, 0:NE], ident[:])
            ins.then_inc(r_cols, 1)
            turn_hidden(0)
            mm(ps[6][0:NE, 0:1], before[0:NE, 0:NE], ext[0:NE, :], start=True, stop=True)
            mm(ps[6][:, 1:2], ones[0:NE, :], ext[0:NE, :], start=True, stop=True).then_inc(r_cols, 1)
            down(0, item_places(0))
            pe.wait_ge(r_sel, 1)
            for t in range(NT):
                o = ps[6][:, t * EXTRA:(t + 1) * EXTRA]
                mm(o, rankT[0:NE, t * P:(t + 1) * P], sel[0:NE, :], start=True, stop=False)
                mm(o, ones[0:NE, :], selb[0:NE, :], start=False, stop=True)
            for t in range(NT):
                mm(ps[6][:, (2 + t) * EXTRA:(3 + t) * EXTRA], weightT[0:NE, t * P:(t + 1) * P], sel[0:NE, :],
                   start=True, stop=True)
            mm(ps[6][:, 4 * EXTRA:5 * EXTRA], part_iota[0:NE, :], sel[0:NE, :], start=True,
               stop=True).then_inc(r_cols, 1)
            pe.wait_ge(r_items, 1)
            for t in range(NT):
                for c in range(2):
                    mm(ps[4 + 2 * t + c][:, :], weightT[0:NE, t * P:(t + 1) * P], bdown[0:NE, c * 512:(c + 1) * 512],
                       start=(t == 1), stop=True, skip_group_check=True)
            n_items = pe.value_load(count_i[0:1, 0:1], min_val=NE, max_val=NE + EXTRA)

            def item(i, places):
                gate_up(i, places)
                scatter_add(i - 1)
                turn_hidden(i)
                gather(6, KD)
                down(i, places)

            with pe.Fori(0, ROUNDS) as j:
                for u in range(ROUND):
                    item(ROUND * j + (1 + u), item_places(1 + u, j))
            residual(1)
            with pe.Fori(NE - 1, n_items) as i:
                item(i, further_places(i))
            pe.wait_ge(tokens_in, n_items + 1)
            for t in range(NT):
                ins = tr(ps[0][:, t * P:(t + 1) * P], onehot_w[:, t, :], ident[:])
            ins.then_inc(sc_turned, 1)
            pe.wait_ge(sc_copied, n_items)
            pe.wait_ge(y_copied, 2 * n_items)
            for t in range(NT):
                scatter_tile(t).then_inc(tile_done, 1)

        @block.vector
        def _(v):
            d = nc.vector
            chain = [0]

            def step(ins):
                chain[0] += 1
                ins.then_inc(dve_chain, 1)
                v.wait_ge(dve_chain, chain[0])

            def half_stats(t, c):
                return d.bn_stats(ln_stats[t][c], hx[:, t, 512 * c:512 * c + 512])

            def normalise(n, t, params=None):
                xt = hx[:, t, :]
                both = tiny.at(12 * t, 12)
                d.bn_aggr(ln_mv[:, t, :], both).then_inc(ln_var, 1)
                v.wait_ge(ln_root, NT * n + t + 1)
                step(d.reciprocal(ln_rstd[:, t:t + 1], ln_std[:, t:t + 1]))
                v.wait_ge(ln_var, NT * n + t + 1)
                if params is None:
                    ins = d.tensor_scalar(xt, xt, ln_mv[:, t, 0:1], ln_rstd[:, t:t + 1], ALU.subtract, ALU.mult)
                else:
                    step(d.scalar_tensor_tensor(out=xt, in0=xt, scalar=ln_mv[:, t, 0:1], in1=params[:, 0, :],
                                                op0=ALU.subtract, op1=ALU.mult))
                    ins = d.scalar_tensor_tensor(out=xt, in0=xt, scalar=ln_rstd[:, t:t + 1], in1=params[:, 1, :],
                                                 op0=ALU.mult, op1=ALU.add)
                ins.then_inc(ln_done, 1)
                v.wait_ge(ln_done, NT * n + t + 1)

            hi_parts = 0
            for s in SCHEDULE:
                kind = s[0]
                if kind == "g":
                    dve_gdn(v, s[1], step)
                    continue
                if kind == "prep":
                    prep_lo(v, d, s[1], "dve")
                    continue
                if kind == "ln":
                    n, t = s[1:]
                    if n == 0:
                        if t == 0:
                            v.wait_ge(x_in, 16)
                            v.wait_ge(lnp_in[0], 32)
                        step(half_stats(t, 0))
                        step(half_stats(t, 1))
                        normalise(0, t, lnp0)
                        if t == 1:
                            v.wait_ge(ab_in, 16)
                            step(d.tensor_copy(w_ab_hi[:], w_ab))
                            d.tensor_tensor(w_ab_lo[:], w_ab, as_f32(w_ab_hi[:]), ALU.subtract).then_inc(ab_split, 2)
                    else:
                        normalise(1, t)
                    continue
                if kind == "ya":
                    v.wait_ge(ya_hi, 1)
                    d.tensor_tensor(src_lo[:, 0:H, :], yaT, as_f32(src_hi[:, 0:H, :]), ALU.subtract).then_inc(ya_split, 1)
                    continue
                if kind == "log decay":
                    v.wait_ge(ab_act, 2)
                    step(d.tensor_tensor(t_c, t_c, t_b, ALU.add))
                    for t in range(NT):
                        ins = d.scalar_tensor_tensor(out=g_log[:, t, :], in0=t_c[:, t, :], scalar=-1.0, in1=ea,
                                                     op0=ALU.mult, op1=ALU.mult)
                    ins.then_inc(g_dve_scal, 1)
                    continue
                if kind == "soft":
                    h = s[1]
                    v.wait_ge(bank_free[bank_of(("score", h))], turn_of(("score", h)))
                    step(d.reciprocal(s_rec[:, h, :], s_sum[:, h, :]))
                    for t in range(NT):
                        ins = d.tensor_scalar(probs[:, h, t, :], probs[:, h, t, :], s_rec[:, h, t:t + 1], None, ALU.mult)
                    ins.then_inc(att_p, 1)
                    continue
                if kind == "sum":
                    c = s[1]
                    v.wait_ge(sum_hi, c + 1)
                    d.tensor_tensor(act_lo[:, c, :], merged[:, c, :], as_f32(act_hi[:, c, :]), ALU.subtract).then_inc(sum_split, 1)
                    continue
                if kind == "sum hi":
                    continue
                bk = ps[bank_of(s)]
                free = bank_free[bank_of(s)]

                def full():
                    v.wait_ge(bank_full[bank_of(s)], turn_of(s))

                if kind in ("memT", "hT", "ym"):
                    hi_parts += 1
                    v.wait_ge(bank_hi, hi_parts)
                    if kind == "memT":
                        hi, lo = (p[:, 2 * s[1]:2 * s[1] + 2, :] for p in (src_hi, src_lo))
                        src = bk[:, :].rearrange("p (a b) -> p a b", a=2)
                    elif kind == "hT":
                        t, j = s[1:]
                        hi, lo = (p[:, 4 * j:4 * j + 4, t * P:(t + 1) * P] for p in (act_hi, act_lo))
                        src = bk[:, :].rearrange("p (a b) -> p a b", b=P)
                    else:
                        hi, lo = (p[:, s[1], :] for p in (src_hi, src_lo))
                        src = bk[:, 0:T]
                    d.tensor_tensor(lo, src, as_f32(hi), ALU.subtract).then_inc(free, 1)
                elif kind == "qkv":
                    c = s[1]
                    v.wait_ge(bank_free[bank_of(s)], turn_of(s))
                    o = qkvT[:, c, :]
                    step(d.tensor_scalar(o, qkv_pad[:, c, 0:T], small_cols[:, c:c + 1], None, ALU.mult))
                    for j in range(1, 4):
                        ins = d.scalar_tensor_tensor(out=o, in0=qkv_pad[:, c, j:j + T], scalar=small_cols[:, 12 * j + c:12 * j + c + 1],
                                                     in1=o, op0=ALU.mult, op1=ALU.add)
                        if j < 3:
                            step(ins)
                    ins.then_inc(conv_done, 1)
                    if c == 11:
                        v.wait_ge(silu_done, 12)
                        d.tensor_tensor(squares, qkvT[:, 0:2 * H, :], qkvT[:, 0:2 * H, :], ALU.mult).then_inc(g_dve_sq, 1)
                elif kind == "ab":
                    v.wait_ge(cols_turned, 1)
                    d.tensor_copy(small_cols[:], ps[3][:, 0:N_ROWS]).then_inc(cols_ready, 1)
                    v.wait_ge(cols_ready, 1)
                    full()
                    d.tensor_copy(ab_rows[0:2 * H, :], bk[0:2 * H, 0:T]).then_inc(free, 1)
                elif kind == "abT":
                    full()
                    v.wait_ge(adt_in, 32)
                    ab = bk[:, 0:NT * 2 * H].rearrange("p (t n) -> p t n", t=NT)
                    for t in range(NT):
                        step(d.tensor_tensor(pre_g[:, t, :], ab[:, t, 0:H], adt[:, 1, :], ALU.add))
                    d.tensor_copy(beta, ab[:, :, H:2 * H]).then_inc(free, 1)
                    v.wait_ge(free, turn_of(s))
                    step(d.tensor_scalar(t_a, pre_g, -1.0, None, ALU.mult))
                    d.tensor_tensor(t_b, t_a, pre_g, ALU.min).then_inc(ab_dve, 1)
                    step(d.tensor_scalar(t_c, pre_g, 0.0, None, ALU.max))
                elif kind == "gc":
                    full()
                    if s[1] == 0:
                        wait_copied(v, "xc", 4)
                        v.wait_ge(pads, 1)
                    d.tensor_tensor(upad[:, s[1], 2:2 + T], bk[:, 0:T], xc[:, s[1], :], ALU.mult).then_inc(free, 1)
                elif kind == "gb":
                    c = s[1]
                    if c == 0:
                        wait_copied(v, "gc", 4)
                    o = xc[:, c, :]
                    step(d.tensor_scalar(o, upad[:, c, 0:T], small_cols[:, 48 + c:49 + c], None, ALU.mult))
                    for j in range(1, 3):
                        step(d.scalar_tensor_tensor(out=o, in0=upad[:, c, j:j + T], scalar=small_cols[:, 48 + 4 * j + c:49 + 4 * j + c],
                                                    in1=o, op0=ALU.mult, op1=ALU.add))
                    v.wait_ge(bank_free[bank_of(s)], turn_of(s))
                    ins = d.tensor_tensor(o, o, gb[:, c, :], ALU.mult)
                    if c == 3:
                        ins.then_inc(yb_ready, 1)
                elif kind == "qm" and s[1] == 1:
                    v.wait_ge(yb_hi, 1)
                    d.tensor_tensor(src_lo[:, H:2 * H, :], xc, as_f32(src_hi[:, H:2 * H, :]), ALU.subtract).then_inc(yb_split, 1)
                elif kind == "score":
                    full()
                    h = s[1]
                    step(d.tensor_reduce(s_max[:, h, :], bk[:, :].rearrange("p (t m) -> p t m", t=NT), AX.X, ALU.max))
                    d.tensor_scalar(s_neg[:, h, :], s_max[:, h, :], -DH ** -0.5, None, ALU.mult).then_inc(att_max, 1)
                elif kind == "br":
                    full()
                    b, c = s[1], s[2]
                    v.wait_ge(bank_free[bank_of(("gate", b, c))], turn_of(("gate", b, c)))
                    m = merged[:, c, :]
                    if b == 2:
                        d.tensor_tensor(m, bk[:, 0:T], first_gates[:, c, :], ALU.mult).then_inc(free, 1)
                    else:
                        gt = gates[:, c, :]
                        d.tensor_tensor(gt, bk[:, 0:T], gt, ALU.mult).then_inc(free, 1)
                        v.wait_ge(free, turn_of(s))
                        d.tensor_tensor(m, m, gt, ALU.add).then_inc(gate_used if b == 1 else sum_ready, 1)
                elif kind == "wo":
                    full()
                    n, t = s[1:]
                    o = hx[:, t, 512 * n:512 * n + 512]
                    d.scalar_tensor_tensor(out=o, in0=o, scalar=ALPHA, in1=bk[:, :], op0=ALU.mult, op1=ALU.add).then_inc(free, 1)
                    v.wait_ge(free, turn_of(s))
                    step(half_stats(t, n))
                elif kind == "x1T" and s[2] == 1:
                    full()
                    t = s[1]
                    for k in range(4, KD):
                        ins = d.tensor_scalar(x1T[:, k, t * P:(t + 1) * P], bk[:, (k - 4) * P:(k - 3) * P],
                                              small_cols[:, ROW_G + k:ROW_G + k + 1], small_cols[:, ROW_B + k:ROW_B + k + 1],
                                              ALU.mult, ALU.add)
                    ins.then_inc(free, 1)
                elif kind == "logits":
                    t = s[1]
                    if t == 0:
                        v.wait_ge(router_in, 32)
                        v.wait_ge(moe_consts, 1)
                    full()
                    d.tensor_tensor(logits[:, t, :], bk[:, 0:NE], br_bc[:], ALU.add).then_inc(free, 1)
                    v.wait_ge(free, turn_of(s))
                    step(d.max(top_v[:, t, :], logits[:, t, :]))
                    step(d.max_index(top_i[:, t, :], top_v[:, t, :], logits[:, t, :]))
                    d.tensor_scalar(r_neg[:, t:t + 1], top_v[:, t, 0:1], -1.0, None, ALU.mult).then_inc(r_max, 1)
                    step(d.tensor_copy(top_f[:, t, :], top_i[:, t, :]))
                    step(d.tensor_scalar(mask[:, t, :], e_iota, top_f[:, t, 0:1], None, ALU.is_equal))
                    for k in range(1, TOPK):
                        ins = d.scalar_tensor_tensor(out=mask[:, t, :], in0=e_iota, scalar=top_f[:, t, k:k + 1],
                                                     in1=mask[:, t, :], op0=ALU.is_equal, op1=ALU.add)
                        if k < TOPK - 1 or t == 0:
                            step(ins)
                    if t == 1:
                        ins.then_inc(r_mask, 1)
                        v.wait_ge(r_mask, 1)
                        v.wait_ge(r_exp, 2)
                        step(d.reciprocal(r_rec, r_sum))
                        for u in range(NT):
                            step(d.scalar_tensor_tensor(out=weights[:, u, 0:NE], in0=el[:, u, :], scalar=r_rec[:, u:u + 1],
                                                        in1=mask[:, u, :], op0=ALU.mult, op1=ALU.mult))
                        step(d.tensor_copy(ids[:, 0:NE], e_iota))
                elif kind == "rank":
                    full()
                    for t in range(NT):
                        step(d.scalar_tensor_tensor(out=ranks[:, t, 0:NE], in0=mask[:, t, :], scalar=-NOT_HERE,
                                                    in1=bk[:, t * NE:(t + 1) * NE], op0=ALU.mult, op1=ALU.add))
                    step(d.tensor_scalar(ranks[:, :, 0:NE], ranks[:, :, 0:NE], NOT_HERE, None, ALU.add))
                    d.tensor_copy(cnt[0:NE, :], bk[0:NE, 2 * NE:2 * NE + 1]).then_inc(free, 1)
                    v.wait_ge(free, turn_of(s))

            def expert_row(i):
                return d.tensor_scalar(e_row[0:NE, :], part_iota[0:NE, 0:CAP], ids[0:NE, bass.ds(i, 1)], None, ALU.is_equal)

            def one_hots(i):
                for t in range(NT):
                    ins = d.tensor_scalar(onehot[:, t, :], slot_iota[:, 0:CAP], ranks[:, t, bass.ds(i, 1)], None, ALU.is_equal)
                ins.then_inc(onehots, 1)

            def weighted_one_hots(i):
                for t in range(NT):
                    d.tensor_scalar(onehot_w[:, t, :], slot_iota, ranks[:, t, bass.ds(i, 1)],
                                    weights[:, t, bass.ds(i, 1)], ALU.is_equal, ALU.mult)

            def copy_tokens():
                d.tensor_copy(x_slotT.rearrange("p a b -> p (a b)"), ps[0][:, :]).then_inc(tokens_in, 1)

            def hidden(i):
                v.wait_ge(gu_done, i + 1)
                d.tensor_scalar(gate1, ps[1][:, :], LIMIT, None, ALU.min).then_inc(gate_cut, 1)
                d.tensor_scalar(up1, ps[2][:, :], LIMIT, -LIMIT, ALU.min, ALU.max).then_inc(up_cut, 1)
                v.wait_ge(up_cut, i + 1)
                v.wait_ge(gate_cut, i + 1)
                d.scalar_tensor_tensor(out=up1, in0=up1, scalar=1.0, in1=gate1, op0=ALU.add, op1=ALU.mult).then_inc(up_gate, 1)
                v.wait_ge(up_gate, i + 1)
                v.wait_ge(sig_done, i + 1)
                d.tensor_tensor(h_tok, up1, sig1, ALU.mult).then_inc(hid_done, 1)

            def copy_y(i):
                v.wait_ge(down_done, i + 1)
                d.tensor_copy(y_tok[64:128, :], ps[3][64:128, :]).then_inc(y_copied, 1)

            def copy_scatter(i):
                v.wait_ge(sc_turned, i + 1)
                d.tensor_copy(scatter, ps[3][:, 0:T]).then_inc(sc_copied, 1)

            expert_row(0)
            one_hots(0)
            v.wait_ge(gathered, 1)
            copy_tokens()
            step(d.tensor_scalar(ext[0:NE, :], cnt[0:NE, :], float(CAP), None, ALU.is_gt))
            for b in (2, 3):
                step(d.tensor_scalar(ext2[0:NE, :], cnt[0:NE, :], float(CAP * b), None, ALU.is_gt))
                step(d.tensor_tensor(ext[0:NE, :], ext[0:NE, :], ext2[0:NE, :], ALU.add))
            one_hots(1)
            weighted_one_hots(0)
            hidden(0)
            expert_row(1)
            v.wait_ge(gathered, 2)
            copy_tokens()
            v.wait_ge(r_cols, 2)
            step(d.tensor_copy(rankT[0:NE, :], ps[7][0:NE, 0:T]))
            step(d.tensor_copy(weightT[0:NE, :], ps[7][0:NE, T:2 * T]))
            step(d.tensor_scalar(q16[0:NE, :], e_iota[0:NE, 0:EXTRA], ps[6][0:NE, 0:1], None, ALU.subtract))
            step(d.tensor_scalar(sel[0:NE, :], q16[0:NE, :], ext[0:NE, :], None, ALU.is_lt))
            step(d.scalar_tensor_tensor(out=sel[0:NE, :], in0=q16[0:NE, :], scalar=0.0, in1=sel[0:NE, :],
                                        op0=ALU.is_ge, op1=ALU.mult))
            step(d.tensor_scalar(q16[0:NE, :], q16[0:NE, :], 1.0, -float(CAP), ALU.add, ALU.mult))
            step(d.tensor_tensor(selb[0:NE, :], q16[0:NE, :], sel[0:NE, :], ALU.mult))
            d.tensor_scalar(count_i[0:1, :], ps[6][0:1, 1:2], float(NE), None, ALU.add).then_inc(r_sel, 1)
            v.wait_ge(r_cols, 3)
            step(d.tensor_copy(ranks[:, :, NE:NE + EXTRA], ps[6][:, 0:2 * EXTRA].rearrange("p (t n) -> p t n", t=NT)))
            step(d.tensor_copy(weights[:, :, NE:NE + EXTRA], ps[6][:, 2 * EXTRA:4 * EXTRA].rearrange("p (t n) -> p t n", t=NT)))
            step(d.tensor_copy(ids[:, NE:NE + EXTRA], ps[6][:, 4 * EXTRA:5 * EXTRA]))
            d.tensor_copy(ids_i[0:1, :], ids[0:1, :]).then_inc(r_items, 1)
            v.wait_ge(r_items, 1)
            copy_y(0)
            n_items = v.value_load(count_i[0:1, 0:1], min_val=NE, max_val=NE + EXTRA)
            with v.Fori(1, n_items) as i:
                one_hots(i + 1)
                copy_scatter(i - 1)
                weighted_one_hots(i)
                hidden(i)
                expert_row(i + 1)
                v.wait_ge(gathered, i + 2)
                copy_tokens()
                copy_y(i)
            v.wait_ge(sc_turned, n_items)
            d.tensor_copy(scatter, ps[0][:, 0:T]).then_inc(sc_copied, 1)
            v.wait_ge(lnp_in[2], 32)
            for t in range(NT):
                v.wait_ge(tile_done, t + 1)
                for c in range(2):
                    ins = d.bn_stats(ln_stats[t][c], ps[4 + 2 * t + c][:, :])
                step(ins)
                d.bn_aggr(ln_mv[:, t, :], tiny.at(12 * t, 12)).then_inc(ln_var, 1)
            for t in range(NT):
                v.wait_ge(ln_var, NT * 2 + t + 1)
                v.wait_ge(ln_root, NT * 2 + t + 1)
                step(d.reciprocal(ln_rstd[:, t:t + 1], ln_std[:, t:t + 1]))
                for c in range(2):
                    o = hx[:, t, 512 * c:512 * c + 512]
                    step(d.scalar_tensor_tensor(out=o, in0=ps[4 + 2 * t + c][:, :], scalar=ln_mv[:, t, 0:1],
                                                in1=lnp2[:, 0, 512 * c:512 * c + 512], op0=ALU.subtract, op1=ALU.mult))
                    d.scalar_tensor_tensor(out=o, in0=o, scalar=ln_rstd[:, t:t + 1],
                                           in1=lnp2[:, 1, 512 * c:512 * c + 512], op0=ALU.mult, op1=ALU.add).then_inc(half_out, 1)


_INS = ['x', 'mem', 'ln0_g', 'ln0_b', 'w_in', 'conv_qkv', 'conv_mix', 'a_log', 'dt_bias', 'gdn_norm',
        'w_mem_kv', 'w_br', 'w_o', 'ln1_g', 'ln1_b', 'w_router', 'b_router', 'w_gate_up', 'b_gate_up',
        'w_down', 'b_down', 'ln2_g', 'ln2_b']
_OUTS = [((1, T, D), 'float32')]


def kernel(**inputs):
    import numpy as _np
    import concourse.bacc as _bacc
    from concourse import mybir as _mybir
    from concourse.bass_utils import run_bass_kernel_spmd as _run

    nc = _bacc.Bacc("TRN2", target_bir_lowering=False, num_devices=1)
    arrays, args = {}, []
    for name in _INS:
        a = _np.ascontiguousarray(inputs[name])
        arrays[f"in_{name}_dram"] = a
        args.append(nc.dram_tensor(f"in_{name}_dram", a.shape, _mybir.dt.from_np(a.dtype), kind="ExternalInput").ap())
    for i, (shape, dtype) in enumerate(_OUTS):
        dt = _mybir.dt.from_np(_np.dtype(dtype))
        args.append(nc.dram_tensor(f"out_{i}_dram", shape, dt, kind="ExternalOutput").ap())
    hybrid_layer(nc, *args)
    r = _run(nc, [arrays], core_ids=[0])
    return r.results[0]["out_0_dram"]
```
